# Optimizing a Trainium2 kernel written in Bass

```python
import math
import jax
import jax.numpy as jnp
from jax import lax
import numpy as np

D_MODEL = 1024
BATCH = 1
SEQ = 1024
DEPTH = 2

CHUNK = 64
Q_BLOCK = 128
SB_HEADS = 4
SB_HEAD_DIM = 64
SB_WIDTH = SB_HEADS * SB_HEAD_DIM
SSM_HEADS = 8
SSM_HEAD_DIM = 64
SSM_WIDTH = SSM_HEADS * SSM_HEAD_DIM
SSM_GROUPS = 2
SSM_STATE = 64
SSM_CONV = 4
SSM_CONV_DIM = SSM_WIDTH + 2 * SSM_GROUPS * SSM_STATE
SC_WIDTH = 256
SC_CONV = 3
MIX_WIDTH = SB_WIDTH + SSM_WIDTH + SC_WIDTH
IN_SEGMENTS = (SB_WIDTH, SB_WIDTH, SB_WIDTH,
               SSM_WIDTH, SSM_CONV_DIM, SSM_HEADS,
               SC_WIDTH, SC_WIDTH, SC_WIDTH)
IN_WIDTH = sum(IN_SEGMENTS)
PEER_HEADS = 4
PEER_KEY_DIM = 256
PEER_NKEYS = 128
PEER_TOPK = 16
PEER_EXPERTS = PEER_NKEYS * PEER_NKEYS
TOKEN_BLOCK = 128
EPS = 1e-6

kernel_name = 'hybrid_stickbreak_ssd_shortconv_peer'

def rmsnorm(x, w):
    x32 = x.astype(jnp.float32)
    y = x32 * lax.rsqrt(jnp.mean(x32 * x32, axis=-1, keepdims=True) + EPS)
    return (y * w.astype(jnp.float32)).astype(x.dtype)

def causal_depthwise_conv(x, w):
    k, c = w.shape
    return lax.conv_general_dilated(
        x, w[:, None, :].astype(x.dtype), window_strides=(1,), padding=[(k - 1, 0)],
        dimension_numbers=('NWC', 'WIO', 'NWC'), feature_group_count=c)

def stick_breaking_attention(q, k, v):
    b, s, h, dh = q.shape
    nblk = s // Q_BLOCK
    scale = dh ** -0.5

    def blocks(a):
        return a.astype(jnp.float32).reshape(b, nblk, Q_BLOCK, h, dh).transpose(1, 0, 3, 2, 4)

    qb, kb, vb = blocks(q), blocks(k), blocks(v)
    qi_np = np.concatenate([np.full(i + 1, i, np.int32) for i in range(nblk)])
    kj_np = np.concatenate([np.arange(i, -1, -1, dtype=np.int32) for i in range(nblk)])
    idx = jnp.arange(Q_BLOCK)
    diag_mask = idx[None, :] < idx[:, None]
    upper = (idx[:, None] > idx[None, :]).astype(jnp.float32)

    def step(carry, ij):
        acc, out_acc, buf = carry
        i, j = ij
        first = j == i
        z = jnp.einsum('bhqd,bhkd->bhqk', qb[i], kb[j]) * scale
        mask = diag_mask | (j < i)
        l = jax.nn.log_sigmoid(-z)
        lm = jnp.where(mask, l, 0.0)
        acc = jnp.where(first, 0.0, acc)
        out_acc = jnp.where(first, 0.0, out_acc)
        rev = jnp.einsum('bhqj,js->bhqs', lm, upper) + acc[..., None]
        w = jnp.where(mask, jnp.exp(l + z + rev), 0.0)
        out_acc = out_acc + jnp.einsum('bhqk,bhkd->bhqd', w, vb[j])
        acc = acc + jnp.sum(lm, axis=-1)
        buf = lax.dynamic_update_index_in_dim(buf, out_acc, i, 0)
        return (acc, out_acc, buf), None

    init = (jnp.zeros((b, h, Q_BLOCK), jnp.float32),
            jnp.zeros((b, h, Q_BLOCK, dh), jnp.float32),
            jnp.zeros((nblk, b, h, Q_BLOCK, dh), jnp.float32))
    (_, _, out), _ = lax.scan(step, init, (jnp.asarray(qi_np), jnp.asarray(kj_np)))
    return out.transpose(1, 0, 3, 2, 4).reshape(b, s, h, dh)

def segsum(x):
    L = x.shape[-1]
    idx = jnp.arange(L)
    xx = jnp.broadcast_to(x[..., :, None], x.shape + (L,))
    xx = jnp.where(idx[:, None] > idx[None, :], xx, 0.0)
    ss = jnp.cumsum(xx, axis=-2)
    return jnp.where(idx[:, None] >= idx[None, :], ss, -jnp.inf)

def ssd_scan(x, dt, A, Bm, Cm):
    b, s, h, p = x.shape
    n = Bm.shape[-1]
    nc = s // CHUNK
    xd = (x * dt[..., None]).reshape(b, nc, CHUNK, h, p)
    a = (dt * A).reshape(b, nc, CHUNK, h).transpose(0, 3, 1, 2)
    Bc = Bm.reshape(b, nc, CHUNK, h, n)
    Cc = Cm.reshape(b, nc, CHUNK, h, n)
    a_cs = jnp.cumsum(a, axis=-1)
    Lmat = jnp.exp(segsum(a))
    cb = jnp.einsum('bclhn,bcshn->bhcls', Cc, Bc)
    y_diag = jnp.einsum('bhcls,bcshp->bclhp', cb * Lmat, xd)
    decay = jnp.exp(a_cs[..., -1:] - a_cs)
    states = jnp.einsum('bclhn,bhcl,bclhp->bchpn', Bc, decay, xd)
    chunk_decay = jnp.exp(a_cs[..., -1])

    def step(carry, inp):
        st, dec = inp
        return carry * dec[..., None, None] + st, carry

    init = jnp.zeros((b, h, p, n), jnp.float32)
    _, prev = lax.scan(step, init, (states.transpose(1, 0, 2, 3, 4), chunk_decay.transpose(2, 0, 1)))
    prev = prev.transpose(1, 0, 2, 3, 4)
    y_off = jnp.einsum('bclhn,bchpn,bhcl->bclhp', Cc, prev, jnp.exp(a_cs))
    return (y_diag + y_off).reshape(b, s, h, p)

def hybrid_mixer(h, w_in, ssm_conv_w, ssm_conv_b, ssm_dt_bias, ssm_A_log, ssm_D, ssm_norm_w, sc_conv_w, w_out):
    b, s, _ = h.shape
    proj = jnp.einsum('bsd,de->bse', h, w_in)
    cuts = []
    acc = 0
    for width in IN_SEGMENTS[:-1]:
        acc += width
        cuts.append(acc)
    q, k, v, z, xbc, dt_raw, sc_b, sc_c, sc_v = jnp.split(proj, cuts, axis=-1)

    y_sb = stick_breaking_attention(q.reshape(b, s, SB_HEADS, SB_HEAD_DIM),
                                    k.reshape(b, s, SB_HEADS, SB_HEAD_DIM),
                                    v.reshape(b, s, SB_HEADS, SB_HEAD_DIM)).reshape(b, s, SB_WIDTH)

    xbc = jax.nn.silu(causal_depthwise_conv(xbc, ssm_conv_w) + ssm_conv_b.astype(xbc.dtype))
    xbc = xbc.astype(jnp.float32)
    xs = xbc[..., :SSM_WIDTH].reshape(b, s, SSM_HEADS, SSM_HEAD_DIM)
    rep = SSM_HEADS // SSM_GROUPS
    Bm = jnp.repeat(xbc[..., SSM_WIDTH:SSM_WIDTH + SSM_GROUPS * SSM_STATE].reshape(b, s, SSM_GROUPS, SSM_STATE), rep, axis=2)
    Cm = jnp.repeat(xbc[..., SSM_WIDTH + SSM_GROUPS * SSM_STATE:].reshape(b, s, SSM_GROUPS, SSM_STATE), rep, axis=2)
    dt = jax.nn.softplus(dt_raw.astype(jnp.float32) + ssm_dt_bias.astype(jnp.float32))
    A = -jnp.exp(ssm_A_log.astype(jnp.float32))
    y_ssm = ssd_scan(xs, dt, A, Bm, Cm) + ssm_D.astype(jnp.float32)[:, None] * xs
    y_ssm = y_ssm.reshape(b, s, SSM_WIDTH) * jax.nn.silu(z.astype(jnp.float32))
    y_ssm = rmsnorm(y_ssm, ssm_norm_w)

    y_sc = sc_b * causal_depthwise_conv(sc_c * sc_v, sc_conv_w)

    y = jnp.concatenate([y_sb.astype(h.dtype), y_ssm.astype(h.dtype), y_sc.astype(h.dtype)], axis=-1)
    return jnp.einsum('bse,ed->bsd', y, w_out)

def peer_ffn(h, w_q, sub_keys, u, v):
    b, s, d = h.shape
    half = PEER_KEY_DIM // 2
    q = jnp.einsum('bsd,de->bse', h, w_q).astype(jnp.float32).reshape(b, s, PEER_HEADS, 2, half)
    scores = jnp.einsum('bshtk,tnk->bshtn', q, sub_keys.astype(jnp.float32))
    s_top, i_top = lax.top_k(scores, PEER_TOPK)
    cand = s_top[..., 0, :, None] + s_top[..., 1, None, :]
    cand_idx = i_top[..., 0, :, None] * PEER_NKEYS + i_top[..., 1, None, :]
    kk = PEER_TOPK * PEER_TOPK
    best, pos = lax.top_k(cand.reshape(b, s, PEER_HEADS, kk), PEER_TOPK)
    expert = jnp.take_along_axis(cand_idx.reshape(b, s, PEER_HEADS, kk), pos, axis=-1)
    gate = jax.nn.softmax(best, axis=-1)

    nblk = s // TOKEN_BLOCK
    hb = h.reshape(b, nblk, TOKEN_BLOCK, d).transpose(1, 0, 2, 3)
    eb = expert.reshape(b, nblk, TOKEN_BLOCK, PEER_HEADS, PEER_TOPK).transpose(1, 0, 2, 3, 4)
    gb = gate.reshape(b, nblk, TOKEN_BLOCK, PEER_HEADS, PEER_TOPK).transpose(1, 0, 2, 3, 4)

    def block(args):
        hx, ex, gx = args
        ue = u[ex]
        act = jax.nn.gelu(jnp.einsum('btd,bthkd->bthk', hx, ue).astype(jnp.float32), approximate=False)
        ve = v[ex]
        return jnp.einsum('bthk,bthkd->btd', (gx * act).astype(ve.dtype), ve)

    out = lax.map(block, (hb, eb, gb))
    return out.transpose(1, 0, 2, 3).reshape(b, s, d).astype(h.dtype)

def setup_inputs(seed: int = 0) -> dict:
    key = jax.random.key(seed)
    ks = jax.random.split(key, 20)
    f32 = jnp.float32

    def nrm(k, shape, scale):
        return jax.random.normal(k, shape, f32) * scale

    dt = jnp.exp(jax.random.uniform(ks[6], (DEPTH, SSM_HEADS), f32, math.log(1e-3), math.log(1e-1)))
    return {
        'x': nrm(ks[0], (BATCH, SEQ, D_MODEL), 1.0),
        'norm1_w': 1.0 + nrm(ks[1], (DEPTH, D_MODEL), 0.05),
        'w_in': nrm(ks[2], (DEPTH, D_MODEL, IN_WIDTH), D_MODEL ** -0.5),
        'ssm_conv_w': nrm(ks[3], (DEPTH, SSM_CONV, SSM_CONV_DIM), SSM_CONV ** -0.5),
        'ssm_conv_b': nrm(ks[4], (DEPTH, SSM_CONV_DIM), 0.02),
        'ssm_dt_bias': dt + jnp.log(-jnp.expm1(-dt)),
        'ssm_A_log': jnp.log(jax.random.uniform(ks[7], (DEPTH, SSM_HEADS), f32, 1.0, 16.0)),
        'ssm_D': 1.0 + nrm(ks[8], (DEPTH, SSM_HEADS), 0.1),
        'ssm_norm_w': 1.0 + nrm(ks[9], (DEPTH, SSM_WIDTH), 0.05),
        'sc_conv_w': nrm(ks[10], (DEPTH, SC_CONV, SC_WIDTH), SC_CONV ** -0.5),
        'w_out': nrm(ks[11], (DEPTH, MIX_WIDTH, D_MODEL), MIX_WIDTH ** -0.5),
        'norm2_w': 1.0 + nrm(ks[12], (DEPTH, D_MODEL), 0.05),
        'peer_w_q': nrm(ks[13], (DEPTH, D_MODEL, PEER_HEADS * PEER_KEY_DIM), D_MODEL ** -0.5),
        'peer_sub_keys': nrm(ks[14], (DEPTH, 2, PEER_NKEYS, PEER_KEY_DIM // 2), (PEER_KEY_DIM // 2) ** -0.5),
        'peer_u': nrm(ks[15], (DEPTH, PEER_EXPERTS, D_MODEL), D_MODEL ** -0.5),
        'peer_v': nrm(ks[16], (DEPTH, PEER_EXPERTS, D_MODEL), 0.5),
        'final_norm_w': 1.0 + nrm(ks[17], (D_MODEL,), 0.05),
    }

def reference(x, norm1_w, w_in, ssm_conv_w, ssm_conv_b, ssm_dt_bias, ssm_A_log, ssm_D, ssm_norm_w,
              sc_conv_w, w_out, norm2_w, peer_w_q, peer_sub_keys, peer_u, peer_v, final_norm_w):
    for i in range(DEPTH):
        h = rmsnorm(x, norm1_w[i])
        x = x + hybrid_mixer(h, w_in[i], ssm_conv_w[i], ssm_conv_b[i], ssm_dt_bias[i], ssm_A_log[i],
                             ssm_D[i], ssm_norm_w[i], sc_conv_w[i], w_out[i])
        h = rmsnorm(x, norm2_w[i])
        x = x + peer_ffn(h, peer_w_q[i], peer_sub_keys[i], peer_u[i], peer_v[i])
    return rmsnorm(x, final_norm_w)


_drawn_inputs = setup_inputs


def setup_inputs(seed=0):
    import zlib

    import numpy as np

    out = dict(_drawn_inputs(seed))
    spreads = {}
    factors = {}
    for name, (base, spread) in spreads.items():
        noise = np.random.default_rng([zlib.crc32(name.encode()), seed]).standard_normal(out[name].shape)
        drawn = base * np.exp(spread * noise) if base else spread * noise
        out[name] = jnp.asarray(drawn.astype(out[name].dtype))
    for name, factor in factors.items():
        out[name] = (out[name] * factor).astype(out[name].dtype)
    return out
```

```python
from contextlib import ExitStack

import concourse.bass as bass
from concourse import mybir

F32 = mybir.dt.float32
U32 = mybir.dt.uint32
ALU = mybir.AluOpType
ACT = mybir.ActivationFunctionType
AX = mybir.AxisListType.X

P = 128
D = 1024
KT = D // P
SEQ, DEPTH = 1024, 2
NB = SEQ // P
ITEMS = NB * DEPTH
IN_W = 2824
Q0, K0, V0, Z0, XBC0, DT0, SB0, SC0, SV0 = 0, 256, 512, 768, 1280, 2048, 2056, 2312, 2568
HD = 64
NH_SB, NH_SSM = 4, 8
NEXP = 16384
TOPK, PH = 16, 4
SLOTS = TOPK * PH
EPS = 1e-6
BIG = 1e30
WS = 2
CHUNKS = 2 * KT
RU, RV, RD = 2, 4, 4
GRP = 8
NG = SLOTS // GRP
CW, CB, SCW, N1, SNW, PKW = 0, 24, 30, 36, 44, 48
DVE_STEPS = 57
ACT_STEPS = 19


def build(nc, x, w_in, w_out, w_q, keys, pk_in, rows_in, norm2, fnorm, cst_in, peer_u, peer_v, stream, out):
    with ExitStack() as ctx:
        def sb(name, shape, dt=F32):
            return ctx.enter_context(nc.sbuf_tensor(name, shape, dt))

        def ps(name, shape):
            return ctx.enter_context(nc.psum_tensor(name, shape, F32))

        def sem(name):
            return ctx.enter_context(nc.semaphore(name))

        win = sb("win", [P, KT, IN_W])
        wst = sb("wst", [P, WS, D])
        keysT = sb("keysT", [P, 2, P])
        pk = sb("pk", [P, PKW])
        rows = sb("rows", [P, 24])
        n2row = sb("n2row", [P, D])
        fnrow = sb("fnrow", [P, D])
        ident = sb("ident", [P, P])
        tri = sb("tri", [P, P])
        cmr = sb("cmr", [P, SEQ])
        cst = sb("cst", [P, ITEMS, 3])
        iota16 = sb("iota16", [P, TOPK])
        eps = sb("eps", [P, 1])
        kT = sb("kT", [P, 2, SEQ])
        vc = sb("vc", [P, NB, 256])
        state = sb("state", [P, 4, HD])
        pre = sb("pre", [P, 6, 3 + P])
        prod = sb("prod", [P, 2, 2 + P])
        xin = sb("xin", [P, D])
        hT = sb("hT", [P, KT, P])
        qT = sb("qT", [P, 2, P])
        xbcT = sb("xbcT", [P, 6, P])
        cur = sb("cur", [P, 3])
        sm = sb("sm", [P, 16])
        dts = sb("dts", [P, 6, 8])
        cd = sb("cd", [P, 8])
        dec = sb("dec", [P, 8])
        negA = sb("negA", [P, 8])
        AR = [sb(f"ar{i}", [P, D]) for i in range(6)]
        cbm = AR[5][:, 0:256].rearrange("p (g l) -> p g l", g=2)
        btok = AR[5][:, 256:384]
        scb = AR[5][:, 384:640].rearrange("p (c t) -> p c t", c=2)
        zs = AR[4][:, 512:1024]
        t8 = sb("t8", [P, 8, TOPK])
        ti = sb("ti", [P, 8, TOPK], U32)
        tf = sb("tf", [P, 8, TOPK])
        bv = sb("bv", [P, PH, TOPK])
        bp = sb("bp", [P, PH, TOPK], U32)
        bab = sb("bab", [P, 2, SLOTS], U32)
        baf = sb("baf", [P, 2, SLOTS])
        eid = sb("eid", [P, 2, SLOTS])
        idxF = sb("idxF", [P, SLOTS], U32)
        gateF = sb("gateF", [P, PH, TOPK])
        gsum = sb("gsum", [P, 2, PH])
        hP = sb("hP", [P, D])
        xP = sb("xP", [P, D])
        idxP = sb("idxP", [P, SLOTS], U32)
        gateP = sb("gateP", [P, SLOTS])
        dots = sb("dots", [P, SLOTS])
        gel = sb("gel", [P, SLOTS])
        wgt = sb("wgt", [P, SLOTS])
        uring = sb("uring", [P, RU, D])
        vring = sb("vring", [P, RV, D])
        diag = sb("diag", [P, RD, P])
        smP = sb("smP", [P, 4])

        pA = ps("pA", [P, D])
        pB = ps("pB", [P, D])
        pC = ps("pC", [P, 512])
        pD = ps("pD", [P, 512])
        acc = ps("acc", [P, D])

        s_boot = sem("s_boot")
        s_tri = sem("s_tri")
        s_const = sem("s_const")
        s_cst = sem("s_cst")
        s_stream = sem("s_stream")
        s_copy = sem("s_copy")
        s_out = sem("s_out")
        s_par = sem("s_par")
        s_win = [sem(f"s_win{k}") for k in range(KT)]
        s_wst = [sem(f"s_wst{k}") for k in range(WS)]
        s_wused = sem("s_wused")
        s_x = sem("s_x")
        s_hand = sem("s_hand")
        s_dve = sem("s_dve")
        s_act = sem("s_act")
        s_fence = sem("s_fence")
        s_ss1, s_xn, s_hTp, s_hTr = sem("s_ss1"), sem("s_xn"), sem("s_hTp"), sem("s_hTr")
        s_proj = sem("s_proj")
        s_hist, s_qk, s_xbc, s_v, s_ez, s_evd = (sem("s_hist"), sem("s_qk"), sem("s_xbc"), sem("s_v"),
                                                 sem("s_ez"), sem("s_evd"))
        s_cpre, s_cexp, s_cT = sem("s_cpre"), sem("s_cexp"), sem("s_cT")
        s_dtr, s_sp, s_a = sem("s_dtr"), sem("s_sp"), sem("s_a")
        s_xtok, s_acs, s_eacs, s_seg, s_L, s_tok = (sem("s_xtok"), sem("s_acs"), sem("s_eacs"), sem("s_seg"),
                                                    sem("s_L"), sem("s_tok"))
        s_G, s_ydg, s_st, s_ys, s_yn, s_ynT = (sem("s_G"), sem("s_ydg"), sem("s_st"), sem("s_ys"),
                                               sem("s_yn"), sem("s_ynT"))
        s_z, s_zm, s_lg, s_cum, s_w, s_wTp, s_wT, s_pv, s_yT = (
            sem("s_z"), sem("s_zm"), sem("s_lg"), sem("s_cum"), sem("s_w"), sem("s_wTp"), sem("s_wT"),
            sem("s_pv"), sem("s_yT"))
        s_ysb = sem("s_ysb")
        s_mix, s_x2, s_xn2, s_h2, s_h2Tp, s_h2T, s_q2T, s_sc = (
            sem("s_mix"), sem("s_x2"), sem("s_xn2"), sem("s_h2"), sem("s_h2Tp"), sem("s_h2T"),
            sem("s_q2T"), sem("s_sc"))
        s_gd, s_ge, s_route = sem("s_gd"), sem("s_ge"), sem("s_route")
        s_lu = [sem(f"s_lu{k}") for k in range(RU)]
        s_lv = [sem(f"s_lv{k}") for k in range(RV)]
        s_free = sem("s_free")
        s_dot, s_gel, s_wgt, s_diag, s_vused = sem("s_dot"), sem("s_gel"), sem("s_wgt"), sem("s_diag"), sem("s_vused")
        s_xo, s_fr, s_fin = sem("s_xo"), sem("s_fr"), sem("s_fin")

        def chain(eng, s, base):
            count = [0]

            def then(ins):
                count[0] += 1
                ins.then_inc(s, 1)
                eng.wait_ge(s, base + count[0])
            return then, count

        def wide(ap, n):
            return ap[:, :, None].to_broadcast((P, ap.shape[1], n))

        def wcols(a, j):
            return win[:, a, j:j + P]

        def load_layer(sp, layer):
            if layer:
                sp.wait_ge(s_proj, 6 * NB)
            for k in range(KT):
                sp.dma_start(win[:, k, :], w_in[layer, :, k, :]).then_inc(s_win[k], 16)
            if layer:
                sp.wait_ge(s_route, NB)
            sp.dma_start(keysT[:, :, :], keys[layer]).then_inc(s_par, 16)
            sp.dma_start(pk[:, :], pk_in[layer]).then_inc(s_par, 16)
            sp.dma_start(rows[:, :], rows_in[layer:layer + 1, :].to_broadcast((P, 24))).then_inc(s_par, 16)
            sp.dma_start(n2row[:, :], norm2[layer:layer + 1, :].to_broadcast((P, D))).then_inc(s_par, 16)

        def mix_loads(sp, m, layer):
            if layer is None:
                sp.dma_start(xin[:, :], x[0:P, :]).then_inc(s_x, 16)
            else:
                if layer:
                    sp.wait_ge(s_stream, 16 * (m - NB + 1))
                    sp.sem_inc(s_fence, 1)
                sp.wait_ge(s_hand, m)
                sp.sem_inc(s_fence, 1)
                sp.dma_start(xin[:, :], stream[bass.ds(m * P, P), :]).then_inc(s_x, 16)
        
        def mix_weights(sp, m, first):
            for c in range(CHUNKS):
                if not (first and c < WS):
                    sp.wait_ge(s_wused, m * CHUNKS + c - WS + 1)
                    sp.sem_inc(s_fence, 1)
                if c < KT:
                    src = w_out[bass.ds((m // NB) * D + c * P, P), :]
                else:
                    src = w_q[bass.ds((m // NB) * D + (c - KT) * P, P), :]
                sp.dma_start(wst[:, c % WS, :], src).then_inc(s_wst[c % WS], 16)

        def peer_stores(sp, n):
            sp.wait_ge(s_xo, n + 1)
            sp.sem_inc(s_fence, 1)
            sp.dma_start(stream[bass.ds((n + NB) * P, P), :], xP[:, :]).then_inc(s_stream, 16)
            sp.wait_ge(s_fin, n + 1)
            sp.sem_inc(s_fence, 1)
            sp.dma_start(out[bass.ds((n % NB) * P, P), :], hP[:, :]).then_inc(s_out, 16)

        def mix_act(act, m):
            then, count = chain(act, s_act, m * ACT_STEPS)

            def root(col, total, width):
                then(act.activation(sm[:, col:col + 1], total, ACT.Ln, scale=1.0 / width, bias=eps[:, 0:1]))
                then(act.activation(sm[:, col:col + 1], sm[:, col:col + 1], ACT.Exp, scale=-0.5))

            act.wait_ge(s_x, 16 * m + 16)
            then(act.activation(AR[0][:, :], xin[:, :], ACT.Square, accum_out=sm[:, 0:1]))
            root(1, sm[:, 0:1], D)
            act.activation(AR[0][:, :], xin[:, :], ACT.Copy, scale=sm[:, 1:2]).then_inc(s_xn, 1)
            act.wait_ge(s_proj, 6 * m + 1)
            act.activation(qT[:, :, :], pC[:, 0:256].rearrange("p (c t) -> p c t", c=2), ACT.Copy,
                           scale=HD ** -0.5).then_inc(s_qk, 1)
            act.activation(kT[:, :, bass.ds((m % NB) * P, P)], pC[:, 256:512].rearrange("p (c t) -> p c t", c=2),
                           ACT.Copy).then_inc(s_qk, 1)
            act.wait_ge(s_hist, m + 1)
            act.wait_ge(s_proj, 6 * m + 2)
            act.activation(pre[:, 0:4, 3:3 + P], pD[:, :].rearrange("p (c t) -> p c t", c=4),
                           ACT.Copy).then_inc(s_xbc, 1)
            act.wait_ge(s_proj, 6 * m + 3)
            act.activation(pre[:, 4:6, 3:3 + P], pB[:, 0:256].rearrange("p (c t) -> p c t", c=2),
                           ACT.Copy).then_inc(s_xbc, 1)
            act.activation(prod[:, :, 2:2 + P], pB[:, 256:512].rearrange("p (c t) -> p c t", c=2),
                           ACT.Copy).then_inc(s_xbc, 1)
            act.wait_ge(s_proj, 6 * m + 5)
            act.activation(dts[:, 0, :], pA[:, 256:264], ACT.Copy)
            act.sem_inc(s_fence, 1)
            act.activation(vc[:, bass.ds(m % NB, 1), :].rearrange("p a c -> p (a c)"), pA[:, 0:256],
                           ACT.Copy).then_inc(s_v, 1)
            act.wait_ge(s_proj, 6 * m + 6)
            act.activation(zs[:, :], pA[:, 512:1024], ACT.Exp, scale=-1.0).then_inc(s_ez, 1)
            act.wait_ge(s_dtr, m + 1)
            then(act.activation(dts[:, 1, :], dts[:, 0, :], ACT.Abs))
            then(act.activation(dts[:, 1, :], dts[:, 1, :], ACT.Exp, scale=-1.0))
            act.activation(negA[:, :], rows[:, 8:16], ACT.Exp)
            act.activation(dts[:, 1, :], dts[:, 1, :], ACT.Ln, bias=1.0).then_inc(s_sp, 1)
            act.wait_ge(s_cpre, m + 1)
            act.activation(AR[1][:, 0:768], AR[0][:, 0:768], ACT.Exp, scale=-1.0).then_inc(s_cexp, 1)
            act.wait_ge(s_seg, m + 1)
            act.activation(dts[:, 5, :], dts[:, 4, :], ACT.Exp)
            act.activation(cd[:, :], cd[:, :], ACT.Exp).then_inc(s_eacs, 1)
            act.activation(AR[2][:, :], AR[2][:, :], ACT.Exp).then_inc(s_L, 1)
            act.wait_ge(s_ys, m + 1)
            then(act.activation(AR[1][:, 0:512], AR[0][:, 0:512], ACT.Square, accum_out=sm[:, 2:3]))
            root(3, sm[:, 2:3], 512)
            act.activation(AR[0][:, 0:512], AR[0][:, 0:512], ACT.Copy, scale=sm[:, 3:4]).then_inc(s_yn, 1)
            for h in range(NH_SB):
                zm, lg = AR[h % 2], AR[2 + h % 2]
                act.wait_ge(s_zm, NH_SB * m + h + 1)
                then(act.activation(lg[:, :], zm[:, :], ACT.Abs))
                then(act.activation(lg[:, :], lg[:, :], ACT.Exp, scale=-1.0))
                act.activation(lg[:, :], lg[:, :], ACT.Ln, bias=1.0).then_inc(s_lg, 1)
                act.wait_ge(s_cum, NH_SB * m + h + 1)
                act.activation(zm[:, :], zm[:, :], ACT.Exp).then_inc(s_w, 1)
                act.wait_ge(s_wTp, NH_SB * m + h + 1)
                act.activation(AR[5][:, :], pB[:, :], ACT.Copy).then_inc(s_wT, 1)
            act.wait_ge(s_pv, NH_SB * (m + 1))
            act.activation(hT[:, 0:2, :], pC[:, 0:256].rearrange("p (c t) -> p c t", c=2),
                           ACT.Copy).then_inc(s_ysb, 1)
            act.wait_ge(s_x2, m + 1)
            then(act.activation(AR[0][:, :], xin[:, :], ACT.Square, accum_out=sm[:, 4:5]))
            root(5, sm[:, 4:5], D)
            act.activation(AR[0][:, :], xin[:, :], ACT.Copy, scale=sm[:, 5:6]).then_inc(s_xn2, 1)
            act.wait_ge(s_h2Tp, m + 1)
            act.activation(hT[:, :, :], pB[:, :].rearrange("p (c t) -> p c t", c=KT), ACT.Copy).then_inc(s_h2T, 1)
            act.wait_ge(s_wused, CHUNKS * m + CHUNKS)
            act.activation(AR[2][:, :], pA[:, :], ACT.Copy).then_inc(s_q2T, 1)
            act.wait_ge(s_gd, m + 1)
            act.activation(gateF[:, :, :], gateF[:, :, :], ACT.Exp).then_inc(s_ge, 1)
            assert count[0] == ACT_STEPS, count

        def mix_pe(pe, m):
            pe.wait_ge(s_xn, m + 1)
            for k in range(KT):
                mm = pe.transpose(pA[:, k * P:(k + 1) * P], AR[0][:, k * P:(k + 1) * P], ident[:, :])
            mm.then_inc(s_hTp, 1)
            pe.wait_ge(s_hTr, m + 1)
            for k in range(KT):
                pe.wait_ge(s_win[k], 16 * (m // NB) + 16)

            def tiles(bank, cols):
                for i, c0 in enumerate(cols):
                    for k in range(KT):
                        mm = pe.matmul(bank[:, i * P:(i + 1) * P], wcols(k, c0), hT[:, k, :],
                                       start=(k == 0), stop=(k == KT - 1))
                mm.then_inc(s_proj, 1)
            tiles(pC[:, :], [Q0, Q0 + P, K0, K0 + P])
            tiles(pD[:, :], [XBC0 + P * i for i in range(4)])
            tiles(pB[:, 0:512], [XBC0 + 4 * P, XBC0 + 5 * P, SC0, SC0 + P])
            tiles(pB[:, 512:1024], [SB0, SB0 + P, SV0, SV0 + P])
            for c0, width, at in ((V0, 256, 0), (DT0, 8, 256), (Z0, 512, 512)):
                for k in range(KT):
                    mm = pe.matmul(pA[:, at:at + width], hT[:, k, :], win[:, k, c0:c0 + width],
                                   start=(k == 0), stop=(k == KT - 1))
                if c0 != V0:
                    mm.then_inc(s_proj, 1)
            pe.wait_ge(s_a, m + 1)
            pe.wait_ge(s_v, m + 1)
            pe.wait_ge(s_evd, m + 1)
            pe.wait_ge(s_xbc, 3 * m + 3)
            pe.matmul(pD[:, 384:392], tri[:, :], dts[:, 3, :], start=True, stop=True)
            for h in range(NH_SSM):
                mm = pe.matmul(pA[:, h * P:(h + 1) * P], dts[:, 3, h:h + 1].to_broadcast((P, P)), tri[:, :],
                               start=True, stop=True)
            mm.then_inc(s_acs, 1)
            pe.wait_ge(s_cT, m + 1)
            pe.wait_ge(s_seg, m + 1)
            pe.wait_ge(s_qk, 2 * m + 2)
            for i in range(4):
                pe.transpose(pC[:, i * P:(i + 1) * P], xbcT[:, i, :], ident[:, :])
            pe.transpose(pD[:, 0:P], xbcT[:, 4, :], ident[:, :])
            for g in range(2):
                lo = g * HD
                mm = pe.matmul((pD, pA)[g][:, P:2 * P], xbcT[lo:lo + HD, 4, :], xbcT[lo:lo + HD, 5, :],
                               start=True, stop=True)
            mm.then_inc(s_xtok, 1)
            pe.wait_ge(s_tok, m + 1)
            for g in range(2):
                lo = g * HD
                pe.matmul((pB, pA)[g][:, 512:768], xbcT[lo:lo + HD, 5, :],
                          state[lo:lo + HD, :, :].rearrange("p h d -> p (h d)"), start=True, stop=True)
            pe.matmul(pC[:, :], btok[:, :], AR[4][:, 0:512], start=True, stop=True).then_inc(s_ydg, 1)
            pe.wait_ge(s_G, m + 1)
            for h in range(NH_SSM):
                mm = pe.matmul(pB[:, h * HD:(h + 1) * HD], AR[2][:, h * P:(h + 1) * P],
                               AR[3][:, h * HD:(h + 1) * HD], start=True, stop=True)
            mm.then_inc(s_ydg, 1)
            def scores(h):
                c, lo = h // 2, HD * (h % 2)
                for j in range(2):
                    mm = pe.matmul(pA[:, j * 512:(j + 1) * 512], qT[lo:lo + HD, c, :],
                                   kT[lo:lo + HD, c, j * 512:(j + 1) * 512], start=True, stop=True)
                mm.then_inc(s_z, 1)
            pe.wait_ge(s_st, m + 1)
            scores(0)
            pe.wait_ge(s_yn, m + 1)
            for i in range(4):
                mm = pe.transpose(pD[:, i * P:(i + 1) * P], AR[0][:, i * P:(i + 1) * P], ident[:, :])
            mm.then_inc(s_ynT, 1)
            for h in range(NH_SB):
                c, lo = h // 2, HD * (h % 2)
                if h + 1 < NH_SB:
                    pe.wait_ge(s_zm, NH_SB * m + h + 1)
                    scores(h + 1)
                pe.wait_ge(s_w, NH_SB * m + h + 1)
                for j in range(NB):
                    mm = pe.transpose(pB[:, j * P:(j + 1) * P], AR[h % 2][:, j * P:(j + 1) * P], ident[:, :])
                mm.then_inc(s_wTp, 1)
                pe.wait_ge(s_wT, NH_SB * m + h + 1)
                for j in range(NB):
                    mm = pe.matmul(pC[lo:lo + HD, c * P:(c + 1) * P], vc[:, j, h * HD:(h + 1) * HD],
                                   AR[5][:, j * P:(j + 1) * P], start=(j == 0), stop=(j == NB - 1))
                mm.then_inc(s_pv, 1)
            pe.wait_ge(s_ysb, m + 1)
            pe.wait_ge(s_yT, m + 1)
            for c in range(KT):
                pe.wait_ge(s_wst[c % WS], 16 * (m * (CHUNKS // WS) + c // WS + 1))
                for j in range(2):
                    mm = pe.matmul(pA[:, j * 512:(j + 1) * 512], hT[:, c, :],
                                   wst[:, c % WS, j * 512:(j + 1) * 512], start=(c == 0), stop=(c == KT - 1))
                mm.then_inc(s_wused, 1)
            pe.wait_ge(s_h2, m + 1)
            for k in range(KT):
                mm = pe.transpose(pB[:, k * P:(k + 1) * P], AR[1][:, k * P:(k + 1) * P], ident[:, :])
            mm.then_inc(s_h2Tp, 1)
            pe.wait_ge(s_h2T, m + 1)
            for j in range(KT):
                c = KT + j
                pe.wait_ge(s_wst[c % WS], 16 * (m * (CHUNKS // WS) + c // WS + 1))
                for k in range(KT):
                    mm = pe.matmul(pA[:, j * P:(j + 1) * P], wst[:, c % WS, k * P:(k + 1) * P], hT[:, k, :],
                                   start=(k == 0), stop=(k == KT - 1))
                mm.then_inc(s_wused, 1)
            pe.wait_ge(s_q2T, m + 1)
            for j in range(KT):
                mm = pe.matmul(pB[:, j * P:(j + 1) * P], AR[2][:, j * P:(j + 1) * P], keysT[:, j % 2, :],
                               start=True, stop=True)
            mm.then_inc(s_sc, 1)

        def mix_dve(dve, m):
            then, count = chain(dve, s_dve, m * DVE_STEPS)
            tt, ts, stt = dve.tensor_tensor, dve.tensor_scalar, dve.scalar_tensor_tensor

            then(ts(cur[:, :], cst[:, bass.ds(m, 1), :].rearrange("p a c -> p (a c)"), 1.0, None, ALU.mult))
            keep, qoff, first_expert = cur[:, 0:1], cur[:, 1:2], cur[:, 2:3]
            ts(state[:, :, :], state[:, :, :], keep, None, ALU.mult)
            ts(prod[:, :, 0:2], prod[:, :, P:P + 2], keep, None, ALU.mult)
            ts(pre[:, :, 0:3], pre[:, :, P:P + 3], keep, None, ALU.mult).then_inc(s_hist, 1)
            dve.wait_ge(s_par, 64 * (m // NB) + 64)
            dve.wait_ge(s_hTp, m + 1)
            tt(hT[:, :, :], pA[:, :].rearrange("p (c t) -> p c t", c=KT), wide(pk[:, N1:N1 + KT], P),
               ALU.mult).then_inc(s_hTr, 1)
            dve.wait_ge(s_xbc, 3 * m + 3)
            dve.wait_ge(s_proj, 6 * m + 4)
            dve.tensor_copy(scb[:, :, :], pB[:, 512:768].rearrange("p (c t) -> p c t", c=2))
            tt(prod[:, :, 2:2 + P], prod[:, :, 2:2 + P], pB[:, 768:1024].rearrange("p (c t) -> p c t", c=2),
               ALU.mult)
            dve.wait_ge(s_v, m + 1)
            tt(dts[:, 0, :], dts[:, 0, :], rows[:, 0:8], ALU.add).then_inc(s_dtr, 1)
            dve.wait_ge(s_ez, m + 1)
            then(ts(zs[:, :], zs[:, :], 1.0, None, ALU.add))
            then(dve.reciprocal(zs[:, :], zs[:, :]))
            tt(zs[:, :], zs[:, :], pA[:, 512:1024], ALU.mult).then_inc(s_evd, 1)
            dve.wait_ge(s_sp, m + 1)
            then(stt(out=dts[:, 2, :], in0=dts[:, 0, :], scalar=0.0, in1=dts[:, 1, :], op0=ALU.max, op1=ALU.add))
            stt(out=dts[:, 3, :], in0=dts[:, 2, :], scalar=-1.0, in1=negA[:, :], op0=ALU.mult,
                op1=ALU.mult).then_inc(s_a, 1)
            c0 = AR[0][:, 0:768].rearrange("p (c t) -> p c t", c=6)
            c1 = AR[1][:, 0:768].rearrange("p (c t) -> p c t", c=6)
            cw = pk[:, CW:CW + 24].rearrange("p (j c) -> p j c", j=4)
            then(tt(c0, pre[:, :, 0:P], wide(cw[:, 0, :], P), ALU.mult))
            for j in range(1, 4):
                then(tt(c1, pre[:, :, j:j + P], wide(cw[:, j, :], P), ALU.mult))
                then(tt(c0, c0, c1, ALU.add))
            tt(c0, c0, wide(pk[:, CB:CB + 6], P), ALU.add).then_inc(s_cpre, 1)
            s0 = AR[4][:, 0:256].rearrange("p (c t) -> p c t", c=2)
            s1 = AR[4][:, 256:512].rearrange("p (c t) -> p c t", c=2)
            sw = pk[:, SCW:SCW + 6].rearrange("p (j c) -> p j c", j=3)
            then(tt(s0, prod[:, :, 0:P], wide(sw[:, 0, :], P), ALU.mult))
            for j in range(1, 3):
                then(tt(s1, prod[:, :, j:j + P], wide(sw[:, j, :], P), ALU.mult))
                then(tt(s0, s0, s1, ALU.add))
            dve.wait_ge(s_proj, 6 * m + 6)
            then(tt(hT[:, 6:8, :], s0, scb[:, :, :], ALU.mult))
            dve.wait_ge(s_cexp, m + 1)
            then(ts(c1, c1, 1.0, None, ALU.add))
            then(dve.reciprocal(c1, c1))
            tt(xbcT[:, :, :], c0, c1, ALU.mult).then_inc(s_cT, 1)
            dve.wait_ge(s_acs, m + 1)
            dve.tensor_copy(cd[:, :], pA[:, P - 1:D:P])
            then(dve.tensor_copy(dts[:, 4, :], pD[:, 384:392]))
            L = AR[2][:, :].rearrange("p (h l) -> p h l", h=NH_SSM)
            then(tt(L, pA[:, :].rearrange("p (h l) -> p h l", h=NH_SSM), wide(dts[:, 4, :], P), ALU.subtract))
            ts(AR[2][:, :], AR[2][:, :], 0.0, None, ALU.min).then_inc(s_seg, 1)
            xt, xd, xdd = AR[3][:, 512:1024], AR[3][:, 0:512], AR[4][:, 0:512]
            h8 = lambda ap: ap.rearrange("p (h d) -> p h d", h=NH_SSM)
            dve.wait_ge(s_xtok, m + 1)
            dve.tensor_copy(btok[:, :], pD[:, 0:P])
            for g in range(2):
                tt(cbm[:, g, :], (pD, pA)[g][:, P:2 * P], tri[:, :], ALU.mult)
            then(dve.tensor_copy(xt, pC[:, :]))
            then(tt(h8(xd), h8(xt), wide(dts[:, 2, :], HD), ALU.mult))
            dve.wait_ge(s_L, m + 1)
            then(dve.tensor_copy(dec[:, :], AR[2][:, P - 1:D:P]))
            tt(h8(xdd), h8(xd), wide(dec[:, :], HD), ALU.mult).then_inc(s_tok, 1)
            for g in range(2):
                half = L[:, 4 * g:4 * g + 4, :]
                ins = tt(half, half, cbm[:, g:g + 1, :].to_broadcast((P, 4, P)), ALU.mult)
            ins.then_inc(s_G, 1)
            y = AR[0][:, 0:512]
            tmp = AR[1][:, 0:512]
            dve.wait_ge(s_ydg, 2 * m + 1)
            dve.wait_ge(s_eacs, m + 1)
            for g in range(2):
                lo = g * HD
                tt(state[lo:lo + HD, :, :], state[lo:lo + HD, :, :],
                   cd[lo:lo + HD, 4 * g:4 * g + 4, None].to_broadcast((HD, 4, HD)), ALU.mult)
            for g in range(2):
                ins = tt(h8(y)[:, 4 * g:4 * g + 4, :], (pB, pA)[g][:, 512:768].rearrange("p (h d) -> p h d", h=4),
                         wide(dts[:, 5, 4 * g:4 * g + 4], HD), ALU.mult)
            then(ins)
            for g in range(2):
                lo = g * HD
                ins = tt(state[lo:lo + HD, :, :], state[lo:lo + HD, :, :],
                         pC[lo:lo + HD, 256 * g:256 * g + 256].rearrange("p (h d) -> p h d", h=4), ALU.add)
            ins.then_inc(s_st, 1)
            then(tt(h8(tmp), h8(xt), wide(rows[:, 16:24], HD), ALU.mult))
            then(tt(y, y, tmp, ALU.add))
            dve.wait_ge(s_ydg, 2 * m + 2)
            then(tt(y, y, pB[:, 0:512], ALU.add))
            tt(y, y, zs[:, :], ALU.mult).then_inc(s_ys, 1)
            dve.wait_ge(s_ynT, m + 1)
            tt(hT[:, 2:6, :], pD[:, :].rearrange("p (c t) -> p c t", c=4), wide(pk[:, SNW:SNW + 4], P),
               ALU.mult).then_inc(s_yT, 1)
            for h in range(NH_SB):
                zm, lg, cum = AR[h % 2], AR[2 + h % 2], AR[4]
                dve.wait_ge(s_z, NH_SB * m + h + 1)
                if h >= 2:
                    dve.wait_ge(s_wTp, NH_SB * m + h - 1)
                stt(out=zm[:, :], in0=cmr[:, :], scalar=qoff, in1=pA[:, :], op0=ALU.add,
                    op1=ALU.min).then_inc(s_zm, 1)
                dve.wait_ge(s_lg, NH_SB * m + h + 1)
                then(stt(out=lg[:, :], in0=zm[:, :], scalar=0.0, in1=lg[:, :], op0=ALU.max, op1=ALU.add))
                then(dve.tensor_tensor_scan(cum[:, ::-1], lg[:, ::-1], lg[:, ::-1], 0.0, ALU.add, ALU.bypass))
                tt(zm[:, :], zm[:, :], cum[:, :], ALU.subtract).then_inc(s_cum, 1)
            dve.wait_ge(s_wused, CHUNKS * m + KT)
            tt(xin[:, :], xin[:, :], pA[:, :], ALU.add).then_inc(s_x2, 1)
            dve.wait_ge(s_xn2, m + 1)
            tt(AR[1][:, :], AR[0][:, :], n2row[:, :], ALU.mult).then_inc(s_h2, 1)
            dve.wait_ge(s_sc, m + 1)
            dve.sem_inc(s_fence, 1)
            pl = [pB[:, j * P:(j + 1) * P] for j in range(8)]
            wk = [AR[3][:, j * P:(j + 1) * P] for j in range(8)]
            top16(dve, then, pl, wk, [t8[:, j, :] for j in range(8)], [ti[:, j, :] for j in range(8)])
            then(dve.tensor_copy(tf[:, :, :], ti[:, :, :]))
            ht = t8[:, :, :].rearrange("p (h t) k -> p h t k", t=2)
            cand = AR[4][:, :].rearrange("p (h i j) -> p h i j", h=PH, i=TOPK)
            sq = (P, PH, TOPK, TOPK)
            for h in range(PH):
                ins = tt(cand[:, h, :, :], t8[:, 2 * h, :, None].to_broadcast((P, TOPK, TOPK)),
                         t8[:, 2 * h + 1, None, :].to_broadcast((P, TOPK, TOPK)), ALU.add)
            then(ins)
            dve.sem_inc(s_fence, 1)
            n2 = TOPK * TOPK
            top16(dve, then, [AR[4][:, h * n2:(h + 1) * n2] for h in range(PH)],
                  [AR[5][:, h * n2:(h + 1) * n2] for h in range(PH)],
                  [bv[:, h, :] for h in range(PH)], [bp[:, h, :] for h in range(PH)])
            tt(gateF[:, :, :], bv[:, :, :], bv[:, :, 0:1].to_broadcast((P, PH, TOPK)), ALU.subtract).then_inc(s_gd, 1)
            bpf = bp[:, :, :].rearrange("p h k -> p (h k)")
            ts(bab[:, 0, :], bpf, 4, None, ALU.logical_shift_right)
            then(ts(bab[:, 1, :], bpf, 15, None, ALU.bitwise_and))
            then(dve.tensor_copy(baf[:, :, :], bab[:, :, :]))
            hot = AR[3][:, :].rearrange("p (s i) -> p s i", s=SLOTS)
            for t in range(2):
                then(tt(hot, wide(baf[:, t, :], TOPK), iota16[:, None, :].to_broadcast((P, SLOTS, TOPK)),
                        ALU.is_equal))
                for h in range(PH):
                    part = hot[:, h * TOPK:(h + 1) * TOPK, :]
                    ins = tt(part, part, tf[:, 2 * h + t, None, :].to_broadcast((P, TOPK, TOPK)), ALU.mult)
                then(ins)
                then(dve.tensor_reduce(eid[:, t, :], hot, AX, ALU.add))
            then(stt(out=eid[:, 0, :], in0=eid[:, 0, :], scalar=float(P), in1=eid[:, 1, :], op0=ALU.mult, op1=ALU.add))
            ts(idxF[:, :], eid[:, 0, :], first_expert, None, ALU.add)
            dve.wait_ge(s_ge, m + 1)
            then(dve.tensor_reduce(gsum[:, 0, :], gateF[:, :, :], AX, ALU.add))
            then(dve.reciprocal(gsum[:, 1, :], gsum[:, 0, :]))
            tt(gateF[:, :, :], gateF[:, :, :], wide(gsum[:, 1, :], TOPK), ALU.mult).then_inc(s_route, 1)
            assert count[0] == DVE_STEPS, count

        def top16(dve, then, src, work, vals, idxs):
            def fenced(ins):
                then(ins)
                dve.sem_inc(s_fence, 1)
            for s, v in zip(src, vals):
                ins = dve.max(v[:, 0:8], s)
            fenced(ins)
            for s, w, v, i in zip(src, work, vals, idxs):
                dve.max_index(i[:, 0:8], v[:, 0:8], s)
                ins = dve.match_replace(w, v[:, 0:8], s, -3.0e38)
            fenced(ins)
            for w, v in zip(work, vals):
                ins = dve.max(v[:, 8:16], w)
            fenced(ins)
            for w, v, i in zip(work, vals, idxs):
                ins = dve.max_index(i[:, 8:16], v[:, 8:16], w)
            then(ins)

        def peer_pool(pool, n, first):
            pool.wait_ge(s_hand, n + 1)
            pool.sem_inc(s_free, 1)
            for g in range(NG + 1):
                for i in range(GRP):
                    if g < NG:
                        k = GRP * g + i
                        if not (first and k < RU):
                            pool.wait_ge(s_dot, SLOTS * n + k - RU + 1)
                            pool.sem_inc(s_free, 1)
                        pool.indirect_dma_start(uring[:, k % RU, :], None, peer_u[:, :],
                                                bass.IndirectOffsetOnAxis(idxP[:, k:k + 1], 0)).then_inc(
                                                    s_lu[k % RU], 16)
                    if g >= 1:
                        k = GRP * (g - 1) + i
                        if not (first and k < RV):
                            pool.wait_ge(s_vused, SLOTS * n + k - RV + 1)
                            pool.sem_inc(s_free, 1)
                        pool.indirect_dma_start(vring[:, k % RV, :], None, peer_v[:, :],
                                                bass.IndirectOffsetOnAxis(idxP[:, k:k + 1], 0)).then_inc(
                                                    s_lv[k % RV], 16)

        def hand_over(dve, n, first):
            dve.wait_ge(s_route, n + 1)
            if not first:
                dve.wait_ge(s_stream, 16 * n)
                dve.wait_ge(s_out, 16 * n)
                dve.wait_ge(s_vused, SLOTS * n)
            dve.tensor_copy(idxP[:, :], idxF[:, :])
            dve.tensor_copy(gateP[:, :], gateF[:, :, :].rearrange("p h k -> p (h k)"))
            dve.tensor_copy(xP[:, :], xin[:, :])
            dve.tensor_copy(hP[:, :], AR[1][:, :]).then_inc(s_hand, 1)
            dve.wait_ge(s_hand, n + 1)

        def weights_dve(dve, n, g):
            s = slice(GRP * g, GRP * (g + 1))
            dve.wait_ge(s_gel, NG * n + g + 1)
            dve.tensor_tensor(wgt[:, s], gel[:, s], gateP[:, s], ALU.mult).then_inc(s_wgt, 1)

        def dot_dve(dve, n, k):
            dve.wait_ge(s_lu[k % RU], 16 * (n * (SLOTS // RU) + k // RU + 1))
            u = uring[:, k % RU, :]
            dve.tensor_tensor_reduce(u, u, hP[:, :], 1.0, 0.0, ALU.mult, ALU.add,
                                     dots[:, k:k + 1]).then_inc(s_dot, 1)

        def back_dve(dve, n):
            for k in range(SLOTS):
                dot_dve(dve, n, k)
                if k >= GRP and k % GRP == 1:
                    weights_dve(dve, n, k // GRP - 1)
            weights_dve(dve, n, NG - 1)
            finish_dve(dve, n)

        def gelu_act(act, n, g):
            s = slice(GRP * g, GRP * (g + 1))
            act.wait_ge(s_dot, SLOTS * n + GRP * (g + 1))
            act.activation(gel[:, s], dots[:, s], ACT.Gelu).then_inc(s_gel, 1)

        def diag_act(act, n, g, first):
            act.wait_ge(s_wgt, NG * n + g + 1)
            for k in range(GRP * g, GRP * (g + 1)):
                if not (first and k < RD):
                    act.wait_ge(s_vused, SLOTS * n + k - RD + 1)
                act.activation(diag[:, k % RD, :], ident[:, :], ACT.Copy, scale=wgt[:, k:k + 1]).then_inc(s_diag, 1)

        def sum_pe(pe, n, g):
            for k in range(GRP * g, GRP * (g + 1)):
                pe.wait_ge(s_diag, SLOTS * n + k + 1)
                pe.wait_ge(s_lv[k % RV], 16 * (n * (SLOTS // RV) + k // RV + 1))
                for j in range(2):
                    mm = pe.matmul(acc[:, j * 512:(j + 1) * 512], diag[:, k % RD, :],
                                   vring[:, k % RV, j * 512:(j + 1) * 512], start=(k == 0), stop=(k == SLOTS - 1))
                mm.then_inc(s_vused, 1)

        def finish_dve(dve, n):
            dve.wait_ge(s_vused, SLOTS * (n + 1))
            dve.tensor_tensor(xP[:, :], xP[:, :], acc[:, :], ALU.add).then_inc(s_xo, 1)
            dve.wait_ge(s_fr, 3 * n + 3)
            dve.scalar_tensor_tensor(out=hP[:, :], in0=xP[:, :], scalar=smP[:, 1:2], in1=fnrow[:, :],
                                     op0=ALU.mult, op1=ALU.mult).then_inc(s_fin, 1)

        def finish_act(act, n):
            act.wait_ge(s_xo, n + 1)
            act.activation(hP[:, :], xP[:, :], ACT.Square, accum_out=smP[:, 0:1]).then_inc(s_fr, 1)
            act.wait_ge(s_fr, 3 * n + 1)
            act.activation(smP[:, 1:2], smP[:, 0:1], ACT.Ln, scale=1.0 / D, bias=eps[:, 0:1]).then_inc(s_fr, 1)
            act.wait_ge(s_fr, 3 * n + 2)
            act.activation(smP[:, 1:2], smP[:, 1:2], ACT.Exp, scale=-0.5).then_inc(s_fr, 1)

        block = ctx.enter_context(nc.Block())

        @block.sync
        def _(sp):
            mix_loads(sp, 0, None)
            sp.dma_start(cst[:, :, :], cst_in[:, :, :]).then_inc(s_cst, 16)
            load_layer(sp, 0)
            sp.dma_start(fnrow[:, :], fnorm[0:1, :].to_broadcast((P, D))).then_inc(s_cst, 16)
            sp.wait_ge(s_boot, 6)
            sp.dma_start(stream[0:SEQ, :], x[:, :]).then_inc(s_copy, 16)
            sp.wait_ge(s_copy, 16)
            mix_weights(sp, 0, True)
            for layer in range(DEPTH):
                with sp.Fori(layer * NB, (layer + 1) * NB - 1) as n:
                    mix_loads(sp, n + 1, layer)
                    mix_weights(sp, n + 1, False)
                    peer_stores(sp, n)
                last = (layer + 1) * NB - 1
                if layer + 1 < DEPTH:
                    load_layer(sp, layer + 1)
                    mix_loads(sp, last + 1, layer + 1)
                    mix_weights(sp, last + 1, False)
                peer_stores(sp, last)
            sp.wait_ge(s_stream, 16 * ITEMS)
            sp.wait_ge(s_out, 16 * ITEMS)

        @block.gpsimd
        def _(pool):
            pool.memset(ident[:, :], 0.0)
            pool.memset(tri[:, :], 1.0)
            pool.memset(kT[:, :, :], 0.0)
            pool.memset(vc[:, :, :], 0.0)
            pool.memset(state[:, :, :], 0.0)
            pool.memset(pre[:, :, :], 0.0)
            pool.memset(prod[:, :, :], 0.0)
            pool.memset(eps[:, :], EPS)
            pool.iota(iota16[:, :], [[1, TOPK]], base=0, channel_multiplier=0,
                      allow_small_or_imprecise_dtypes=True)
            pool.iota(cmr[:, :], [[-1, SEQ]], base=0, channel_multiplier=1,
                      allow_small_or_imprecise_dtypes=True).then_inc(s_tri, 1)
            pool.wait_ge(s_tri, 1)
            pool.affine_select(out=ident[:, :], in_=ident[:, :], compare_op=ALU.not_equal, fill=1.0,
                               base=0, pattern=[[-1, P]], channel_multiplier=1)
            pool.affine_select(out=tri[:, :], in_=tri[:, :], compare_op=ALU.is_ge, fill=0.0,
                               base=0, pattern=[[1, P]], channel_multiplier=-1).then_inc(s_boot, 6)
            peer_pool(pool, 0, True)
            with pool.Fori(1, ITEMS) as n:
                peer_pool(pool, n, False)

        @block.vector
        def _(dve):
            dve.wait_ge(s_boot, 6)
            dve.tensor_scalar(cmr[:, :], cmr[:, :], -0.5, BIG, ALU.add, ALU.mult).then_inc(s_const, 1)
            dve.wait_ge(s_const, 1)
            dve.wait_ge(s_cst, 32)

            mix_dve(dve, 0)
            hand_over(dve, 0, True)
            with dve.Fori(0, ITEMS - 1) as n:
                back_dve(dve, n)
                mix_dve(dve, n + 1)
                hand_over(dve, n + 1, False)
            back_dve(dve, ITEMS - 1)

        @block.scalar
        def _(act):
            def back(n, first):
                for g in range(NG):
                    gelu_act(act, n, g)
                    diag_act(act, n, g, first)
                finish_act(act, n)
            act.wait_ge(s_boot, 6)
            mix_act(act, 0)
            back(0, True)
            mix_act(act, 1)
            with act.Fori(1, ITEMS - 1) as n:
                back(n, False)
                mix_act(act, n + 1)
            back(ITEMS - 1, False)

        @block.tensor
        def _(pe):
            pe.wait_ge(s_boot, 6)
            mix_pe(pe, 0)
            with pe.Fori(0, ITEMS - 1) as n:
                for g in range(NG):
                    sum_pe(pe, n, g)
                mix_pe(pe, n + 1)
            for g in range(NG):
                sum_pe(pe, ITEMS - 1, g)


def kernel(**inputs):
    import numpy as np
    import concourse.bacc as bacc
    from concourse import mybir
    from concourse.bass_utils import run_bass_kernel_spmd as run

    a = {k: np.asarray(v) for k, v in inputs.items()}

    def tiles(v):
        return v.reshape(DEPTH, -1, P).transpose(0, 2, 1)

    conv = a["ssm_conv_w"].reshape(DEPTH, 4, 6, P).transpose(0, 3, 1, 2).reshape(DEPTH, P, 24)
    short = a["sc_conv_w"].reshape(DEPTH, 3, 2, P).transpose(0, 3, 1, 2).reshape(DEPTH, P, 6)
    item = np.arange(ITEMS)
    cst = np.stack([item % NB != 0, (item % NB) * P * BIG, (item // NB) * NEXP], -1).astype(np.float32)
    arrays = {
        "x": a["x"].reshape(SEQ, D),
        "w_in": a["w_in"].reshape(DEPTH, KT, P, IN_W).transpose(0, 2, 1, 3),
        "w_out": a["w_out"].reshape(DEPTH * D, D),
        "w_q": a["peer_w_q"].reshape(DEPTH, KT, P, KT, P).transpose(0, 3, 2, 1, 4).reshape(DEPTH * D, D),
        "keys": a["peer_sub_keys"].transpose(0, 3, 1, 2),
        "pk": np.concatenate([conv, tiles(a["ssm_conv_b"]), short, tiles(a["norm1_w"]),
                              tiles(a["ssm_norm_w"])], -1),
        "rows": np.concatenate([a["ssm_dt_bias"], a["ssm_A_log"], a["ssm_D"]], -1),
        "norm2": a["norm2_w"],
        "fnorm": a["final_norm_w"].reshape(1, D),
        "cst": np.broadcast_to(cst, (P, ITEMS, 3)),
        "peer_u": a["peer_u"].reshape(DEPTH * NEXP, D),
        "peer_v": a["peer_v"].reshape(DEPTH * NEXP, D),
    }
    arrays = {f"in_{k}": np.ascontiguousarray(v) for k, v in arrays.items()}
    nc = bacc.Bacc("TRN2", target_bir_lowering=False, num_devices=1)
    args = [nc.dram_tensor(k, v.shape, mybir.dt.from_np(v.dtype), kind="ExternalInput").ap()
            for k, v in arrays.items()]
    stream = nc.dram_tensor("stream", ((ITEMS + NB) * P, D), F32, kind="Internal").ap()
    out = nc.dram_tensor("out", (SEQ, D), F32, kind="ExternalOutput").ap()
    build(nc, *args, stream, out)
    result = run(nc, [arrays], core_ids=[0])
    return result.results[0]["out"].reshape(1, SEQ, D)
```

```python
from contextlib import ExitStack

import concourse.bass as bass
from concourse import mybir

F32 = mybir.dt.float32
U32 = mybir.dt.uint32
ALU = mybir.AluOpType
ACT = mybir.ActivationFunctionType
AX = mybir.AxisListType.X

P = 128
D = 1024
KT = D // P
SEQ, DEPTH = 1024, 2
NB = SEQ // P
ITEMS = NB * DEPTH
IN_W = 2824
Q0, K0, V0, Z0, XBC0, DT0, SB0, SC0, SV0 = 0, 256, 512, 768, 1280, 2048, 2056, 2312, 2568
HD = 64
NH_SB, NH_SSM = 4, 8
NEXP = 16384
TOPK, PH = 16, 4
SLOTS = TOPK * PH
EPS = 1e-6
BIG = 1e30
WS = 2
CHUNKS = 2 * KT
RU, RV, RD = 2, 4, 4
GRP = 8
NG = SLOTS // GRP
VD = RV - 1
NVD, NVP = SLOTS // RV, SLOTS // RV * (RV - 1)
CW, CB, SCW, N1, SNW, PKW = 0, 24, 30, 36, 44, 48
DVE_STEPS = 58
ACT_STEPS = 19


def build(nc, x, w_in, w_out, w_q, keys, pk_in, rows_in, norm2, fnorm, cst_in, peer_u, peer_v, stream, out):
    with ExitStack() as ctx:
        def sb(name, shape, dt=F32):
            return ctx.enter_context(nc.sbuf_tensor(name, shape, dt))

        def ps(name, shape):
            return ctx.enter_context(nc.psum_tensor(name, shape, F32))

        def sem(name):
            return ctx.enter_context(nc.semaphore(name))

        win = sb("win", [P, KT, IN_W])
        wst = sb("wst", [P, WS, D])
        keysT = sb("keysT", [P, 2, P])
        pk = sb("pk", [P, PKW])
        rows = sb("rows", [P, 24])
        n2row = sb("n2row", [P, D])
        fnrow = sb("fnrow", [P, D])
        ident = sb("ident", [P, P])
        tri = sb("tri", [P, P])
        cmr = sb("cmr", [P, SEQ])
        cst = sb("cst", [P, ITEMS, 3])
        iota16 = sb("iota16", [P, TOPK])
        eps = sb("eps", [P, 1])
        kT = sb("kT", [P, 2, SEQ])
        vc = sb("vc", [P, NB, 256])
        state = sb("state", [P, 4, HD])
        pre = sb("pre", [P, 6, 3 + P])
        prod = sb("prod", [P, 2, 2 + P])
        xin = sb("xin", [P, D])
        hT = sb("hT", [P, KT, P])
        qT = sb("qT", [P, 2, P])
        xbcT = sb("xbcT", [P, 6, P])
        cur = sb("cur", [P, 3])
        sm = sb("sm", [P, 16])
        dts = sb("dts", [P, 6, 8])
        cd = sb("cd", [P, 8])
        dec = sb("dec", [P, 8])
        negA = sb("negA", [P, 8])
        AR = [sb(f"ar{i}", [P, D]) for i in range(6)]
        cbm = AR[5][:, 0:256].rearrange("p (g l) -> p g l", g=2)
        btok = AR[5][:, 256:384]
        scb = AR[5][:, 384:640].rearrange("p (c t) -> p c t", c=2)
        zs = AR[4][:, 512:1024]
        t8 = sb("t8", [P, 8, TOPK])
        ti = sb("ti", [P, 8, TOPK], U32)
        tf = sb("tf", [P, 8, TOPK])
        bv = sb("bv", [P, PH, TOPK])
        bp = sb("bp", [P, PH, TOPK], U32)
        bab = sb("bab", [P, 2, SLOTS], U32)
        baf = sb("baf", [P, 2, SLOTS])
        eid = sb("eid", [P, 2, SLOTS])
        idxF = sb("idxF", [P, SLOTS], U32)
        gateF = sb("gateF", [P, PH, TOPK])
        gsum = sb("gsum", [P, 2, PH])
        hP = sb("hP", [P, D])
        xP = sb("xP", [P, D])
        idxP = sb("idxP", [P, SLOTS], U32)
        gateP = sb("gateP", [P, SLOTS])
        dots = sb("dots", [P, SLOTS])
        gel = sb("gel", [P, SLOTS])
        wgt = sb("wgt", [P, SLOTS])
        uring = sb("uring", [P, RU, D])
        vring = sb("vring", [P, RV, D])
        diag = sb("diag", [P, RD, P])
        smP = sb("smP", [P, 4])

        pA = ps("pA", [P, D])
        pB = ps("pB", [P, D])
        pC = ps("pC", [P, 512])
        pD = ps("pD", [P, 512])
        acc = ps("acc", [P, D])

        s_boot = sem("s_boot")
        s_tri = sem("s_tri")
        s_const = sem("s_const")
        s_cst = sem("s_cst")
        s_stream = sem("s_stream")
        s_copy = sem("s_copy")
        s_out = sem("s_out")
        s_par = sem("s_par")
        s_win = [sem(f"s_win{k}") for k in range(KT)]
        s_wst = [sem(f"s_wst{k}") for k in range(WS)]
        s_wused = sem("s_wused")
        s_x = sem("s_x")
        s_hand = sem("s_hand")
        s_dve = sem("s_dve")
        s_act = sem("s_act")
        s_fence = sem("s_fence")
        s_ss1, s_xn, s_hTp, s_hTr = sem("s_ss1"), sem("s_xn"), sem("s_hTp"), sem("s_hTr")
        s_proj = sem("s_proj")
        s_hist, s_qk, s_xbc, s_v, s_ez, s_evd = (sem("s_hist"), sem("s_qk"), sem("s_xbc"), sem("s_v"),
                                                 sem("s_ez"), sem("s_evd"))
        s_cpre, s_cexp, s_cT = sem("s_cpre"), sem("s_cexp"), sem("s_cT")
        s_dtr, s_sp, s_a = sem("s_dtr"), sem("s_sp"), sem("s_a")
        s_xtok, s_acs, s_eacs, s_seg, s_L, s_tok = (sem("s_xtok"), sem("s_acs"), sem("s_eacs"), sem("s_seg"),
                                                    sem("s_L"), sem("s_tok"))
        s_G, s_ydg, s_st, s_ys, s_yn, s_ynT = (sem("s_G"), sem("s_ydg"), sem("s_st"), sem("s_ys"),
                                               sem("s_yn"), sem("s_ynT"))
        s_z, s_zm, s_lg, s_cum, s_w, s_wTp, s_wT, s_pv, s_yT = (
            sem("s_z"), sem("s_zm"), sem("s_lg"), sem("s_cum"), sem("s_w"), sem("s_wTp"), sem("s_wT"),
            sem("s_pv"), sem("s_yT"))
        s_ysb = sem("s_ysb")
        s_mix, s_x2, s_xn2, s_h2, s_h2Tp, s_h2T, s_q2T, s_sc = (
            sem("s_mix"), sem("s_x2"), sem("s_xn2"), sem("s_h2"), sem("s_h2Tp"), sem("s_h2T"),
            sem("s_q2T"), sem("s_sc"))
        s_gd, s_ge, s_route = sem("s_gd"), sem("s_ge"), sem("s_route")
        s_lu = [sem(f"s_lu{k}") for k in range(RU)]
        s_lv = [sem(f"s_lv{k}") for k in range(RV)]
        s_free = sem("s_free")
        s_dot, s_gel, s_wgt, s_diag, s_vused = sem("s_dot"), sem("s_gel"), sem("s_wgt"), sem("s_diag"), sem("s_vused")
        s_vdve = sem("s_vdve")
        s_xo, s_fr, s_fin = sem("s_xo"), sem("s_fr"), sem("s_fin")

        def chain(eng, s, base):
            count = [0]

            def then(ins):
                count[0] += 1
                ins.then_inc(s, 1)
                eng.wait_ge(s, base + count[0])
            return then, count

        def wide(ap, n):
            return ap[:, :, None].to_broadcast((P, ap.shape[1], n))

        def wcols(a, j):
            return win[:, a, j:j + P]

        def load_layer(sp, layer):
            if layer:
                sp.wait_ge(s_proj, 6 * NB)
            for k in range(KT):
                sp.dma_start(win[:, k, :], w_in[layer, :, k, :]).then_inc(s_win[k], 16)
            if layer:
                sp.wait_ge(s_route, NB)
            sp.dma_start(keysT[:, :, :], keys[layer]).then_inc(s_par, 16)
            sp.dma_start(pk[:, :], pk_in[layer]).then_inc(s_par, 16)
            sp.dma_start(rows[:, :], rows_in[layer:layer + 1, :].to_broadcast((P, 24))).then_inc(s_par, 16)
            sp.dma_start(n2row[:, :], norm2[layer:layer + 1, :].to_broadcast((P, D))).then_inc(s_par, 16)

        def mix_loads(sp, m, layer):
            if layer is None:
                sp.dma_start(xin[:, :], x[0:P, :]).then_inc(s_x, 16)
            else:
                if layer:
                    sp.wait_ge(s_stream, 16 * (m - NB + 1))
                    sp.sem_inc(s_fence, 1)
                sp.wait_ge(s_hand, m)
                sp.sem_inc(s_fence, 1)
                sp.dma_start(xin[:, :], stream[bass.ds(m * P, P), :]).then_inc(s_x, 16)
        
        def mix_weights(sp, m, first):
            for c in range(CHUNKS):
                if not (first and c < WS):
                    sp.wait_ge(s_wused, m * CHUNKS + c - WS + 1)
                    sp.sem_inc(s_fence, 1)
                if c < KT:
                    src = w_out[bass.ds((m // NB) * D + c * P, P), :]
                else:
                    src = w_q[bass.ds((m // NB) * D + (c - KT) * P, P), :]
                sp.dma_start(wst[:, c % WS, :], src).then_inc(s_wst[c % WS], 16)

        def peer_stores(sp, n):
            sp.wait_ge(s_xo, n + 1)
            sp.sem_inc(s_fence, 1)
            sp.dma_start(stream[bass.ds((n + NB) * P, P), :], xo).then_inc(s_stream, 16)
            sp.wait_ge(s_fin, n + 1)
            sp.sem_inc(s_fence, 1)
            sp.dma_start(out[bass.ds((n % NB) * P, P), :], fin).then_inc(s_out, 16)

        def mix_act(act, m):
            then, count = chain(act, s_act, m * ACT_STEPS)

            def root(col, total, width):
                then(act.activation(sm[:, col:col + 1], total, ACT.Ln, scale=1.0 / width, bias=eps[:, 0:1]))
                then(act.activation(sm[:, col:col + 1], sm[:, col:col + 1], ACT.Exp, scale=-0.5))

            act.wait_ge(s_x, 16 * m + 16)
            then(act.activation(AR[0][:, :], xin[:, :], ACT.Square, accum_out=sm[:, 0:1]))
            root(1, sm[:, 0:1], D)
            act.activation(AR[0][:, :], xin[:, :], ACT.Copy, scale=sm[:, 1:2]).then_inc(s_xn, 1)
            yield 0
            act.wait_ge(s_proj, 6 * m + 1)
            act.activation(qT[:, :, :], pC[:, 0:256].rearrange("p (c t) -> p c t", c=2), ACT.Copy,
                           scale=HD ** -0.5).then_inc(s_qk, 1)
            act.activation(kT[:, :, bass.ds((m % NB) * P, P)], pC[:, 256:512].rearrange("p (c t) -> p c t", c=2),
                           ACT.Copy).then_inc(s_qk, 1)
            act.wait_ge(s_hist, m + 1)
            act.wait_ge(s_proj, 6 * m + 2)
            act.activation(pre[:, 0:4, 3:3 + P], pD[:, :].rearrange("p (c t) -> p c t", c=4),
                           ACT.Copy).then_inc(s_xbc, 1)
            act.wait_ge(s_proj, 6 * m + 3)
            act.activation(pre[:, 4:6, 3:3 + P], pB[:, 0:256].rearrange("p (c t) -> p c t", c=2),
                           ACT.Copy).then_inc(s_xbc, 1)
            act.activation(prod[:, :, 2:2 + P], pB[:, 256:512].rearrange("p (c t) -> p c t", c=2),
                           ACT.Copy).then_inc(s_xbc, 1)
            yield 3
            act.wait_ge(s_cpre, m + 1)
            act.activation(AR[1][:, 0:768], AR[0][:, 0:768], ACT.Exp, scale=-1.0).then_inc(s_cexp, 1)
            yield 7
            act.wait_ge(s_proj, 6 * m + 5)
            act.activation(dts[:, 0, :], pA[:, 256:264], ACT.Copy)
            act.sem_inc(s_fence, 1)
            act.activation(vc[:, bass.ds(m % NB, 1), :].rearrange("p a c -> p (a c)"), pA[:, 0:256],
                           ACT.Copy).then_inc(s_v, 1)
            act.wait_ge(s_dtr, m + 1)
            then(act.activation(dts[:, 1, :], dts[:, 0, :], ACT.Abs))
            then(act.activation(dts[:, 1, :], dts[:, 1, :], ACT.Exp, scale=-1.0))
            act.activation(negA[:, :], rows[:, 8:16], ACT.Exp)
            act.activation(dts[:, 1, :], dts[:, 1, :], ACT.Ln, bias=1.0).then_inc(s_sp, 1)
            yield 11
            act.wait_ge(s_proj, 6 * m + 6)
            act.activation(zs[:, :], pA[:, 512:1024], ACT.Exp, scale=-1.0).then_inc(s_ez, 1)
            yield 13
            act.wait_ge(s_seg, m + 1)
            act.activation(dts[:, 5, :], dts[:, 4, :], ACT.Exp)
            act.activation(cd[:, :], cd[:, :], ACT.Exp).then_inc(s_eacs, 1)
            act.activation(AR[2][:, :], AR[2][:, :], ACT.Exp).then_inc(s_L, 1)
            yield 16
            act.wait_ge(s_ys, m + 1)
            then(act.activation(AR[1][:, 0:512], AR[0][:, 0:512], ACT.Square, accum_out=sm[:, 2:3]))
            root(3, sm[:, 2:3], 512)
            act.activation(AR[0][:, 0:512], AR[0][:, 0:512], ACT.Copy, scale=sm[:, 3:4]).then_inc(s_yn, 1)
            def log_part(h):
                zm, lg = AR[h % 2], AR[2 + h % 2]
                act.wait_ge(s_zm, NH_SB * m + h + 1)
                then(act.activation(lg[:, :], zm[:, :], ACT.Abs))
                then(act.activation(lg[:, :], lg[:, :], ACT.Exp, scale=-1.0))
                act.activation(lg[:, :], lg[:, :], ACT.Ln, bias=1.0).then_inc(s_lg, 1)

            yield 18
            log_part(0)
            for h in range(NH_SB):
                yield 19 + 3 * h
                act.wait_ge(s_cum, NH_SB * m + h + 1)
                act.activation(AR[h % 2][:, :], AR[h % 2][:, :], ACT.Exp).then_inc(s_w, 1)
                yield 20 + 3 * h
                if h + 1 < NH_SB:
                    log_part(h + 1)
                yield 21 + 3 * h
                act.wait_ge(s_wTp, NH_SB * m + h + 1)
                act.activation(AR[5][:, :], pB[:, :], ACT.Copy).then_inc(s_wT, 1)
            yield 31
            act.wait_ge(s_pv, NH_SB * (m + 1))
            act.activation(hT[:, 0:2, :], pC[:, 0:256].rearrange("p (c t) -> p c t", c=2),
                           ACT.Copy).then_inc(s_ysb, 1)
            yield 37
            act.wait_ge(s_x2, m + 1)
            then(act.activation(AR[0][:, :], xin[:, :], ACT.Square, accum_out=sm[:, 4:5]))
            root(5, sm[:, 4:5], D)
            act.activation(AR[0][:, :], xin[:, :], ACT.Copy, scale=sm[:, 5:6]).then_inc(s_xn2, 1)
            yield 38
            act.wait_ge(s_h2Tp, m + 1)
            act.activation(hT[:, :, :], pB[:, :].rearrange("p (c t) -> p c t", c=KT), ACT.Copy).then_inc(s_h2T, 1)
            yield 47
            act.wait_ge(s_wused, CHUNKS * m + CHUNKS)
            act.activation(AR[2][:, :], pA[:, :], ACT.Copy).then_inc(s_q2T, 1)
            yield SLOTS
            act.wait_ge(s_gd, m + 1)
            act.activation(gateF[:, :, :], gateF[:, :, :], ACT.Exp).then_inc(s_ge, 1)
            assert count[0] == ACT_STEPS, count

        def mix_pe(pe, m):
            pe.wait_ge(s_xn, m + 1)
            for k in range(KT):
                mm = pe.transpose(pA[:, k * P:(k + 1) * P], AR[0][:, k * P:(k + 1) * P], ident[:, :])
            mm.then_inc(s_hTp, 1)
            pe.wait_ge(s_hTr, m + 1)
            for k in range(KT):
                pe.wait_ge(s_win[k], 16 * (m // NB) + 16)

            def tiles(bank, cols, row=0):
                for i, c0 in enumerate(cols):
                    yield row + i if row else 0
                    for k in range(KT):
                        mm = pe.matmul(bank[:, i * P:(i + 1) * P], wcols(k, c0), hT[:, k, :],
                                       start=(k == 0), stop=(k == KT - 1))
                mm.then_inc(s_proj, 1)
            yield from tiles(pC[:, :], [Q0, Q0 + P, K0, K0 + P])
            yield from tiles(pD[:, :], [XBC0 + P * i for i in range(4)])
            yield from tiles(pB[:, 0:512], [XBC0 + 4 * P, XBC0 + 5 * P, SC0, SC0 + P])
            yield from tiles(pB[:, 512:1024], [SB0, SB0 + P, SV0, SV0 + P], 1)
            for c0, width, at, row in ((V0, 256, 0, 4), (DT0, 8, 256, 6), (Z0, 512, 512, 6)):
                for k in range(KT):
                    yield row + width * k // 1024
                    mm = pe.matmul(pA[:, at:at + width], hT[:, k, :], win[:, k, c0:c0 + width],
                                   start=(k == 0), stop=(k == KT - 1))
                if c0 != V0:
                    mm.then_inc(s_proj, 1)
            yield 11
            pe.wait_ge(s_a, m + 1)
            pe.wait_ge(s_v, m + 1)
            pe.wait_ge(s_evd, m + 1)
            pe.wait_ge(s_xbc, 3 * m + 3)
            pe.matmul(pD[:, 384:392], tri[:, :], dts[:, 3, :], start=True, stop=True)
            for h in range(NH_SSM):
                mm = pe.matmul(pA[:, h * P:(h + 1) * P], dts[:, 3, h:h + 1].to_broadcast((P, P)), tri[:, :],
                               start=True, stop=True)
            mm.then_inc(s_acs, 1)
            yield 12
            pe.wait_ge(s_cT, m + 1)
            pe.wait_ge(s_seg, m + 1)
            pe.wait_ge(s_qk, 2 * m + 2)
            for i in range(4):
                pe.transpose(pC[:, i * P:(i + 1) * P], xbcT[:, i, :], ident[:, :])
            pe.transpose(pD[:, 0:P], xbcT[:, 4, :], ident[:, :])
            for g in range(2):
                lo = g * HD
                mm = pe.matmul((pD, pA)[g][:, P:2 * P], xbcT[lo:lo + HD, 4, :], xbcT[lo:lo + HD, 5, :],
                               start=True, stop=True)
            mm.then_inc(s_xtok, 1)
            yield 13
            pe.wait_ge(s_tok, m + 1)
            for g in range(2):
                lo = g * HD
                pe.matmul((pB, pA)[g][:, 512:768], xbcT[lo:lo + HD, 5, :],
                          state[lo:lo + HD, :, :].rearrange("p h d -> p (h d)"), start=True, stop=True)
            pe.matmul(pC[:, :], btok[:, :], AR[4][:, 0:512], start=True, stop=True).then_inc(s_ydg, 1)
            yield 14
            pe.wait_ge(s_G, m + 1)
            for h in range(NH_SSM):
                mm = pe.matmul(pB[:, h * HD:(h + 1) * HD], AR[2][:, h * P:(h + 1) * P],
                               AR[3][:, h * HD:(h + 1) * HD], start=True, stop=True)
            mm.then_inc(s_ydg, 1)
            def scores(h):
                c, lo = h // 2, HD * (h % 2)
                for j in range(2):
                    mm = pe.matmul(pA[:, j * 512:(j + 1) * 512], qT[lo:lo + HD, c, :],
                                   kT[lo:lo + HD, c, j * 512:(j + 1) * 512], start=True, stop=True)
                mm.then_inc(s_z, 1)
            yield 15
            pe.wait_ge(s_st, m + 1)
            scores(0)
            yield 17
            pe.wait_ge(s_yn, m + 1)
            for i in range(4):
                mm = pe.transpose(pD[:, i * P:(i + 1) * P], AR[0][:, i * P:(i + 1) * P], ident[:, :])
            mm.then_inc(s_ynT, 1)
            for h in range(NH_SB):
                c, lo = h // 2, HD * (h % 2)
                yield 17 + 3 * h
                if h + 1 < NH_SB:
                    pe.wait_ge(s_zm, NH_SB * m + h + 1)
                    scores(h + 1)
                yield 18 + 3 * h
                pe.wait_ge(s_w, NH_SB * m + h + 1)
                for j in range(NB):
                    mm = pe.transpose(pB[:, j * P:(j + 1) * P], AR[h % 2][:, j * P:(j + 1) * P], ident[:, :])
                mm.then_inc(s_wTp, 1)
                yield 19 + 3 * h
                pe.wait_ge(s_wT, NH_SB * m + h + 1)
                for j in range(NB):
                    mm = pe.matmul(pC[lo:lo + HD, c * P:(c + 1) * P], vc[:, j, h * HD:(h + 1) * HD],
                                   AR[5][:, j * P:(j + 1) * P], start=(j == 0), stop=(j == NB - 1))
                mm.then_inc(s_pv, 1)
            yield 28
            pe.wait_ge(s_ysb, m + 1)
            pe.wait_ge(s_yT, m + 1)
            for c in range(KT):
                yield 28 + c
                pe.wait_ge(s_wst[c % WS], 16 * (m * (CHUNKS // WS) + c // WS + 1))
                for j in range(2):
                    mm = pe.matmul(pA[:, j * 512:(j + 1) * 512], hT[:, c, :],
                                   wst[:, c % WS, j * 512:(j + 1) * 512], start=(c == 0), stop=(c == KT - 1))
                mm.then_inc(s_wused, 1)
            yield 37
            pe.wait_ge(s_h2, m + 1)
            for k in range(KT):
                mm = pe.transpose(pB[:, k * P:(k + 1) * P], AR[1][:, k * P:(k + 1) * P], ident[:, :])
            mm.then_inc(s_h2Tp, 1)
            pe.wait_ge(s_h2T, m + 1)
            for j in range(KT):
                c = KT + j
                yield 38 + j
                pe.wait_ge(s_wst[c % WS], 16 * (m * (CHUNKS // WS) + c // WS + 1))
                for k in range(KT):
                    mm = pe.matmul(pA[:, j * P:(j + 1) * P], wst[:, c % WS, k * P:(k + 1) * P], hT[:, k, :],
                                   start=(k == 0), stop=(k == KT - 1))
                mm.then_inc(s_wused, 1)
            yield 47
            pe.wait_ge(s_q2T, m + 1)
            for j in range(KT):
                mm = pe.matmul(pB[:, j * P:(j + 1) * P], AR[2][:, j * P:(j + 1) * P], keysT[:, j % 2, :],
                               start=True, stop=True)
            mm.then_inc(s_sc, 1)

        def mix_dve(dve, m):
            then, count = chain(dve, s_dve, m * DVE_STEPS)
            tt, ts, stt = dve.tensor_tensor, dve.tensor_scalar, dve.scalar_tensor_tensor

            then(ts(cur[:, :], cst[:, bass.ds(m, 1), :].rearrange("p a c -> p (a c)"), 1.0, None, ALU.mult))
            keep, qoff, first_expert = cur[:, 0:1], cur[:, 1:2], cur[:, 2:3]
            ts(state[:, :, :], state[:, :, :], keep, None, ALU.mult)
            ts(prod[:, :, 0:2], prod[:, :, P:P + 2], keep, None, ALU.mult)
            ts(pre[:, :, 0:3], pre[:, :, P:P + 3], keep, None, ALU.mult).then_inc(s_hist, 1)
            dve.wait_ge(s_par, 64 * (m // NB) + 64)
            yield 2
            dve.wait_ge(s_hTp, m + 1)
            tt(hT[:, :, :], pA[:, :].rearrange("p (c t) -> p c t", c=KT), wide(pk[:, N1:N1 + KT], P),
               ALU.mult).then_inc(s_hTr, 1)
            c0 = AR[0][:, 0:768].rearrange("p (c t) -> p c t", c=6)
            c1 = AR[1][:, 0:768].rearrange("p (c t) -> p c t", c=6)
            cw = pk[:, CW:CW + 24].rearrange("p (j c) -> p j c", j=4)
            yield 9
            dve.wait_ge(s_xbc, 3 * m + 3)
            then(tt(c0, pre[:, :, 0:P], wide(cw[:, 0, :], P), ALU.mult))
            for j in range(1, 4):
                then(tt(c1, pre[:, :, j:j + P], wide(cw[:, j, :], P), ALU.mult))
                then(tt(c0, c0, c1, ALU.add))
                yield 9 + j
            tt(c0, c0, wide(pk[:, CB:CB + 6], P), ALU.add).then_inc(s_cpre, 1)
            yield 13
            dve.wait_ge(s_proj, 6 * m + 4)
            dve.tensor_copy(scb[:, :, :], pB[:, 512:768].rearrange("p (c t) -> p c t", c=2))
            then(tt(prod[:, :, 2:2 + P], prod[:, :, 2:2 + P], pB[:, 768:1024].rearrange("p (c t) -> p c t", c=2),
                    ALU.mult))
            yield 14
            dve.wait_ge(s_cexp, m + 1)
            then(ts(c1, c1, 1.0, None, ALU.add))
            then(dve.reciprocal(c1, c1))
            yield 15
            tt(xbcT[:, :, :], c0, c1, ALU.mult).then_inc(s_cT, 1)
            yield 16
            dve.wait_ge(s_v, m + 1)
            tt(dts[:, 0, :], dts[:, 0, :], rows[:, 0:8], ALU.add).then_inc(s_dtr, 1)
            s0 = AR[4][:, 0:256].rearrange("p (c t) -> p c t", c=2)
            s1 = AR[4][:, 256:512].rearrange("p (c t) -> p c t", c=2)
            sw = pk[:, SCW:SCW + 6].rearrange("p (j c) -> p j c", j=3)
            then(tt(s0, prod[:, :, 0:P], wide(sw[:, 0, :], P), ALU.mult))
            for j in range(1, 3):
                then(tt(s1, prod[:, :, j:j + P], wide(sw[:, j, :], P), ALU.mult))
                then(tt(s0, s0, s1, ALU.add))
            yield 17
            dve.wait_ge(s_sp, m + 1)
            then(stt(out=dts[:, 2, :], in0=dts[:, 0, :], scalar=0.0, in1=dts[:, 1, :], op0=ALU.max, op1=ALU.add))
            stt(out=dts[:, 3, :], in0=dts[:, 2, :], scalar=-1.0, in1=negA[:, :], op0=ALU.mult,
                op1=ALU.mult).then_inc(s_a, 1)
            yield 19
            dve.wait_ge(s_ez, m + 1)
            then(ts(zs[:, :], zs[:, :], 1.0, None, ALU.add))
            then(dve.reciprocal(zs[:, :], zs[:, :]))
            tt(zs[:, :], zs[:, :], pA[:, 512:1024], ALU.mult).then_inc(s_evd, 1)
            then(tt(hT[:, 6:8, :], s0, scb[:, :, :], ALU.mult))
            yield 20
            dve.wait_ge(s_acs, m + 1)
            dve.tensor_copy(cd[:, :], pA[:, P - 1:D:P])
            then(dve.tensor_copy(dts[:, 4, :], pD[:, 384:392]))
            L = AR[2][:, :].rearrange("p (h l) -> p h l", h=NH_SSM)
            then(tt(L, pA[:, :].rearrange("p (h l) -> p h l", h=NH_SSM), wide(dts[:, 4, :], P), ALU.subtract))
            ts(AR[2][:, :], AR[2][:, :], 0.0, None, ALU.min).then_inc(s_seg, 1)
            yield 22
            xt, xd, xdd = AR[3][:, 512:1024], AR[3][:, 0:512], AR[4][:, 0:512]
            h8 = lambda ap: ap.rearrange("p (h d) -> p h d", h=NH_SSM)
            dve.wait_ge(s_xtok, m + 1)
            dve.tensor_copy(btok[:, :], pD[:, 0:P])
            for g in range(2):
                tt(cbm[:, g, :], (pD, pA)[g][:, P:2 * P], tri[:, :], ALU.mult)
            then(dve.tensor_copy(xt, pC[:, :]))
            then(tt(h8(xd), h8(xt), wide(dts[:, 2, :], HD), ALU.mult))
            yield 22
            dve.wait_ge(s_L, m + 1)
            then(dve.tensor_copy(dec[:, :], AR[2][:, P - 1:D:P]))
            tt(h8(xdd), h8(xd), wide(dec[:, :], HD), ALU.mult).then_inc(s_tok, 1)
            for g in range(2):
                half = L[:, 4 * g:4 * g + 4, :]
                ins = tt(half, half, cbm[:, g:g + 1, :].to_broadcast((P, 4, P)), ALU.mult)
            ins.then_inc(s_G, 1)
            yield 23
            y = AR[0][:, 0:512]
            tmp = AR[1][:, 0:512]
            dve.wait_ge(s_ydg, 2 * m + 1)
            dve.wait_ge(s_eacs, m + 1)
            for g in range(2):
                lo = g * HD
                tt(state[lo:lo + HD, :, :], state[lo:lo + HD, :, :],
                   cd[lo:lo + HD, 4 * g:4 * g + 4, None].to_broadcast((HD, 4, HD)), ALU.mult)
            for g in range(2):
                ins = tt(h8(y)[:, 4 * g:4 * g + 4, :], (pB, pA)[g][:, 512:768].rearrange("p (h d) -> p h d", h=4),
                         wide(dts[:, 5, 4 * g:4 * g + 4], HD), ALU.mult)
            then(ins)
            for g in range(2):
                lo = g * HD
                ins = tt(state[lo:lo + HD, :, :], state[lo:lo + HD, :, :],
                         pC[lo:lo + HD, 256 * g:256 * g + 256].rearrange("p (h d) -> p h d", h=4), ALU.add)
            ins.then_inc(s_st, 1)
            then(tt(h8(tmp), h8(xt), wide(rows[:, 16:24], HD), ALU.mult))
            then(tt(y, y, tmp, ALU.add))
            yield 24
            dve.wait_ge(s_ydg, 2 * m + 2)
            then(tt(y, y, pB[:, 0:512], ALU.add))
            tt(y, y, zs[:, :], ALU.mult).then_inc(s_ys, 1)
            def masked(h):
                dve.wait_ge(s_z, NH_SB * m + h + 1)
                if h >= 2:
                    dve.wait_ge(s_wTp, NH_SB * m + h - 1)
                stt(out=AR[h % 2][:, :], in0=cmr[:, :], scalar=qoff, in1=pA[:, :], op0=ALU.add,
                    op1=ALU.min).then_inc(s_zm, 1)

            yield 26
            dve.wait_ge(s_ynT, m + 1)
            tt(hT[:, 2:6, :], pD[:, :].rearrange("p (c t) -> p c t", c=4), wide(pk[:, SNW:SNW + 4], P),
               ALU.mult).then_inc(s_yT, 1)
            masked(0)
            for h in range(NH_SB):
                zm, lg, cum = AR[h % 2], AR[2 + h % 2], AR[4]
                yield 27 + 3 * h
                dve.wait_ge(s_lg, NH_SB * m + h + 1)
                then(stt(out=lg[:, :], in0=zm[:, :], scalar=0.0, in1=lg[:, :], op0=ALU.max, op1=ALU.add))
                yield 28 + 3 * h
                then(dve.tensor_tensor_scan(cum[:, ::-1], lg[:, ::-1], lg[:, ::-1], 0.0, ALU.add, ALU.bypass))
                tt(zm[:, :], zm[:, :], cum[:, :], ALU.subtract).then_inc(s_cum, 1)
                yield 29 + 3 * h
                if h + 1 < NH_SB:
                    masked(h + 1)
            yield 45
            dve.wait_ge(s_wused, CHUNKS * m + KT)
            tt(xin[:, :], xin[:, :], pA[:, :], ALU.add).then_inc(s_x2, 1)
            yield 46
            dve.wait_ge(s_xn2, m + 1)
            tt(AR[1][:, :], AR[0][:, :], n2row[:, :], ALU.mult).then_inc(s_h2, 1)
            yield 56
            dve.wait_ge(s_sc, m + 1)
            dve.sem_inc(s_fence, 1)
            pl = [pB[:, j * P:(j + 1) * P] for j in range(8)]
            wk = [AR[3][:, j * P:(j + 1) * P] for j in range(8)]
            yield from top16(57, dve, then, pl, wk, [t8[:, j, :] for j in range(8)], [ti[:, j, :] for j in range(8)])
            then(dve.tensor_copy(tf[:, :, :], ti[:, :, :]))
            ht = t8[:, :, :].rearrange("p (h t) k -> p h t k", t=2)
            cand = AR[4][:, :].rearrange("p (h i j) -> p h i j", h=PH, i=TOPK)
            sq = (P, PH, TOPK, TOPK)
            for h in range(PH):
                ins = tt(cand[:, h, :, :], t8[:, 2 * h, :, None].to_broadcast((P, TOPK, TOPK)),
                         t8[:, 2 * h + 1, None, :].to_broadcast((P, TOPK, TOPK)), ALU.add)
            then(ins)
            dve.sem_inc(s_fence, 1)
            n2 = TOPK * TOPK
            yield from top16(SLOTS - 1, dve, then, [AR[4][:, h * n2:(h + 1) * n2] for h in range(PH)],
                  [AR[5][:, h * n2:(h + 1) * n2] for h in range(PH)],
                  [bv[:, h, :] for h in range(PH)], [bp[:, h, :] for h in range(PH)])
            yield 68
            tt(gateF[:, :, :], bv[:, :, :], bv[:, :, 0:1].to_broadcast((P, PH, TOPK)), ALU.subtract).then_inc(s_gd, 1)
            bpf = bp[:, :, :].rearrange("p h k -> p (h k)")
            ts(bab[:, 0, :], bpf, 4, None, ALU.logical_shift_right)
            then(ts(bab[:, 1, :], bpf, 15, None, ALU.bitwise_and))
            then(dve.tensor_copy(baf[:, :, :], bab[:, :, :]))
            hot = AR[3][:, :].rearrange("p (s i) -> p s i", s=SLOTS)
            for t in range(2):
                yield 70 + t
                then(tt(hot, wide(baf[:, t, :], TOPK), iota16[:, None, :].to_broadcast((P, SLOTS, TOPK)),
                        ALU.is_equal))
                for h in range(PH):
                    part = hot[:, h * TOPK:(h + 1) * TOPK, :]
                    ins = tt(part, part, tf[:, 2 * h + t, None, :].to_broadcast((P, TOPK, TOPK)), ALU.mult)
                then(ins)
                then(dve.tensor_reduce(eid[:, t, :], hot, AX, ALU.add))
            then(stt(out=eid[:, 0, :], in0=eid[:, 0, :], scalar=float(P), in1=eid[:, 1, :], op0=ALU.mult, op1=ALU.add))
            ts(idxF[:, :], eid[:, 0, :], first_expert, None, ALU.add)
            yield SLOTS + GRP + 1
            dve.wait_ge(s_ge, m + 1)
            then(dve.tensor_reduce(gsum[:, 0, :], gateF[:, :, :], AX, ALU.add))
            then(dve.reciprocal(gsum[:, 1, :], gsum[:, 0, :]))
            tt(gateF[:, :, :], gateF[:, :, :], wide(gsum[:, 1, :], TOPK), ALU.mult).then_inc(s_route, 1)
            assert count[0] == DVE_STEPS, count

        def top16(row, dve, then, src, work, vals, idxs):
            def fenced(ins):
                then(ins)
                dve.sem_inc(s_fence, 1)
            for s, v in zip(src, vals):
                ins = dve.max(v[:, 0:8], s)
            fenced(ins)
            yield row + 1
            for s, w, v, i in zip(src, work, vals, idxs):
                dve.max_index(i[:, 0:8], v[:, 0:8], s)
                ins = dve.match_replace(w, v[:, 0:8], s, -3.0e38)
            fenced(ins)
            yield row + 2
            for w, v in zip(work, vals):
                ins = dve.max(v[:, 8:16], w)
            fenced(ins)
            yield row + 3
            for w, v, i in zip(work, vals, idxs):
                ins = dve.max_index(i[:, 8:16], v[:, 8:16], w)
            then(ins)

        def pe_rows(k):
            return k // RV * (RV - 1) + k % RV

        def gather(pool, ring, slot, table, k, landed):
            pool.indirect_dma_start(ring[:, slot, :], None, table[:, :],
                                    bass.IndirectOffsetOnAxis(idxP[:, k:k + 1], 0)).then_inc(landed[slot], 16)

        def peer_pool(pool, n, first):
            pool.wait_ge(s_hand, n + 1)
            pool.sem_inc(s_free, 1)
            for step in range(SLOTS + GRP):
                k = step
                if k < SLOTS:
                    if not (first and k < RU):
                        pool.wait_ge(s_dot, SLOTS * n + k - RU + 1)
                        pool.sem_inc(s_free, 1)
                    gather(pool, uring, k % RU, peer_u, k, s_lu)
                k = step - GRP
                if k >= 0:
                    if not first and k == 0:
                        pool.wait_ge(s_out, 16 * n)
                        pool.wait_ge(s_stream, 16 * n)
                        pool.sem_inc(s_free, 1)
                    elif k % RV == VD and not (first and k < RV):
                        pool.wait_ge(s_vdve, NVD * n + k // RV)
                        pool.sem_inc(s_free, 1)
                    elif k >= RV:
                        pool.wait_ge(s_vused, NVP * n + pe_rows(k - RV) + 1)
                        pool.sem_inc(s_free, 1)
                    gather(pool, vring, k % RV, peer_v, k, s_lv)

        def hand_over(dve, n, first):
            dve.wait_ge(s_route, n + 1)
            dve.tensor_copy(idxP[:, :], idxF[:, :])
            dve.tensor_copy(gateP[:, :], gateF[:, :, :].rearrange("p h k -> p (h k)"))
            dve.tensor_copy(xP[:, :], xin[:, :])
            dve.tensor_copy(hP[:, :], AR[1][:, :]).then_inc(s_hand, 1)
            dve.wait_ge(s_hand, n + 1)

        def v_landed(eng, n, k):
            eng.wait_ge(s_lv[k % RV], 16 * (n * (SLOTS // RV) + k // RV + 1))

        def weights_dve(dve, n, g):
            s = slice(GRP * g, GRP * (g + 1))
            dve.wait_ge(s_gel, NG * n + g + 1)
            dve.tensor_tensor(wgt[:, s], gel[:, s], gateP[:, s], ALU.mult).then_inc(s_wgt, 1)

        def back_dve(dve, n, k):
            if k < SLOTS:
                dve.wait_ge(s_lu[k % RU], 16 * (n * (SLOTS // RU) + k // RU + 1))
                u = uring[:, k % RU, :]
                dve.tensor_tensor_reduce(u, u, hP[:, :], 1.0, 0.0, ALU.mult, ALU.add,
                                         dots[:, k:k + 1]).then_inc(s_dot, 1)
            v = k - GRP - 1
            if v >= 0 and v % GRP == 0:
                weights_dve(dve, n, v // GRP)
            if v >= 0 and v % RV == VD:
                v_landed(dve, n, v)
                dve.wait_ge(s_wgt, NG * n + v // GRP + 1)
                if v >= RV:
                    dve.wait_ge(s_vdve, NVD * n + v // RV)
                dve.scalar_tensor_tensor(out=xP[:, :], in0=vring[:, VD, :], scalar=wgt[:, v:v + 1], in1=xP[:, :],
                                         op0=ALU.mult, op1=ALU.add).then_inc(s_vdve, 1)

        def back_act(act, n, k, first):
            g = k // GRP
            if k % GRP == 0:
                s = slice(GRP * g, GRP * (g + 1))
                act.wait_ge(s_dot, SLOTS * n + GRP * (g + 1))
                act.activation(gel[:, s], dots[:, s], ACT.Gelu).then_inc(s_gel, 1)
            if k % RV != VD:
                r = pe_rows(k)
                act.wait_ge(s_wgt, NG * n + g + 1)
                if not (first and r < RD):
                    act.wait_ge(s_vused, NVP * n + r - RD + 1)
                act.activation(diag[:, r % RD, :], ident[:, :], ACT.Copy, scale=wgt[:, k:k + 1]).then_inc(s_diag, 1)

        def back_pe(pe, n, k):
            if k % RV != VD:
                r = pe_rows(k)
                pe.wait_ge(s_diag, NVP * n + r + 1)
                v_landed(pe, n, k)
                for j in range(2):
                    mm = pe.matmul(acc[:, j * 512:(j + 1) * 512], diag[:, r % RD, :],
                                   vring[:, k % RV, j * 512:(j + 1) * 512], start=(r == 0), stop=(r == NVP - 1))
                mm.then_inc(s_vused, 1)

        xo, fin = vring[:, 0, :], vring[:, 1, :]

        def finish_dve(dve, n):
            dve.wait_ge(s_vused, NVP * (n + 1))
            dve.wait_ge(s_vdve, NVD * (n + 1))
            dve.tensor_tensor(xo, xP[:, :], acc[:, :], ALU.add).then_inc(s_xo, 1)
            dve.wait_ge(s_xo, n + 1)

        def norm_dve(dve, n):
            dve.wait_ge(s_fr, 3 * n + 3)
            dve.scalar_tensor_tensor(out=fin, in0=xo, scalar=smP[:, 1:2], in1=fnrow[:, :],
                                     op0=ALU.mult, op1=ALU.mult).then_inc(s_fin, 1)

        def finish_act(act, n):
            act.wait_ge(s_xo, n + 1)
            act.activation(fin, xo, ACT.Square, accum_out=smP[:, 0:1]).then_inc(s_fr, 1)
            act.wait_ge(s_fr, 3 * n + 1)
            act.activation(smP[:, 1:2], smP[:, 0:1], ACT.Ln, scale=1.0 / D, bias=eps[:, 0:1]).then_inc(s_fr, 1)
            act.wait_ge(s_fr, 3 * n + 2)
            act.activation(smP[:, 1:2], smP[:, 1:2], ACT.Exp, scale=-0.5).then_inc(s_fr, 1)

        def alone(front):
            for _ in front:
                pass

        def weave(front, back, rows):
            k = 0
            for row in front:
                while k < min(row, rows):
                    back(k)
                    k += 1
            while k < rows:
                back(k)
                k += 1

        block = ctx.enter_context(nc.Block())

        @block.sync
        def _(sp):
            mix_loads(sp, 0, None)
            sp.dma_start(cst[:, :, :], cst_in[:, :, :]).then_inc(s_cst, 16)
            load_layer(sp, 0)
            sp.dma_start(fnrow[:, :], fnorm[0:1, :].to_broadcast((P, D))).then_inc(s_cst, 16)
            sp.wait_ge(s_boot, 6)
            sp.dma_start(stream[0:SEQ, :], x[:, :]).then_inc(s_copy, 16)
            sp.wait_ge(s_copy, 16)
            mix_weights(sp, 0, True)
            for layer in range(DEPTH):
                with sp.Fori(layer * NB, (layer + 1) * NB - 1) as n:
                    mix_loads(sp, n + 1, layer)
                    mix_weights(sp, n + 1, False)
                    peer_stores(sp, n)
                last = (layer + 1) * NB - 1
                if layer + 1 < DEPTH:
                    load_layer(sp, layer + 1)
                    mix_loads(sp, last + 1, layer + 1)
                    mix_weights(sp, last + 1, False)
                peer_stores(sp, last)
            sp.wait_ge(s_stream, 16 * ITEMS)
            sp.wait_ge(s_out, 16 * ITEMS)

        @block.gpsimd
        def _(pool):
            pool.memset(ident[:, :], 0.0)
            pool.memset(tri[:, :], 1.0)
            pool.memset(kT[:, :, :], 0.0)
            pool.memset(vc[:, :, :], 0.0)
            pool.memset(state[:, :, :], 0.0)
            pool.memset(pre[:, :, :], 0.0)
            pool.memset(prod[:, :, :], 0.0)
            pool.memset(eps[:, :], EPS)
            pool.iota(iota16[:, :], [[1, TOPK]], base=0, channel_multiplier=0,
                      allow_small_or_imprecise_dtypes=True)
            pool.iota(cmr[:, :], [[-1, SEQ]], base=0, channel_multiplier=1,
                      allow_small_or_imprecise_dtypes=True).then_inc(s_tri, 1)
            pool.wait_ge(s_tri, 1)
            pool.affine_select(out=ident[:, :], in_=ident[:, :], compare_op=ALU.not_equal, fill=1.0,
                               base=0, pattern=[[-1, P]], channel_multiplier=1)
            pool.affine_select(out=tri[:, :], in_=tri[:, :], compare_op=ALU.is_ge, fill=0.0,
                               base=0, pattern=[[1, P]], channel_multiplier=-1).then_inc(s_boot, 6)
            peer_pool(pool, 0, True)
            with pool.Fori(1, ITEMS) as n:
                peer_pool(pool, n, False)

        @block.vector
        def _(dve):
            dve.wait_ge(s_boot, 6)
            dve.tensor_scalar(cmr[:, :], cmr[:, :], -0.5, BIG, ALU.add, ALU.mult).then_inc(s_const, 1)
            dve.wait_ge(s_const, 1)
            dve.wait_ge(s_cst, 32)

            last = SLOTS + GRP + 1
            alone(mix_dve(dve, 0))
            hand_over(dve, 0, True)
            weave(mix_dve(dve, 1), lambda k: back_dve(dve, 0, k), last)
            finish_dve(dve, 0)
            hand_over(dve, 1, False)
            norm_dve(dve, 0)
            with dve.Fori(1, ITEMS - 1) as n:
                weave(mix_dve(dve, n + 1), lambda k: back_dve(dve, n, k), last)
                finish_dve(dve, n)
                hand_over(dve, n + 1, False)
                norm_dve(dve, n)
            weave((), lambda k: back_dve(dve, ITEMS - 1, k), last)
            finish_dve(dve, ITEMS - 1)
            norm_dve(dve, ITEMS - 1)

        @block.scalar
        def _(act):
            act.wait_ge(s_boot, 6)
            alone(mix_act(act, 0))
            weave(mix_act(act, 1), lambda k: back_act(act, 0, k, True), SLOTS)
            finish_act(act, 0)
            with act.Fori(1, ITEMS - 1) as n:
                weave(mix_act(act, n + 1), lambda k: back_act(act, n, k, False), SLOTS)
                finish_act(act, n)
            weave((), lambda k: back_act(act, ITEMS - 1, k, False), SLOTS)
            finish_act(act, ITEMS - 1)

        @block.tensor
        def _(pe):
            pe.wait_ge(s_boot, 6)
            alone(mix_pe(pe, 0))
            with pe.Fori(0, ITEMS - 1) as n:
                weave(mix_pe(pe, n + 1), lambda k: back_pe(pe, n, k), SLOTS)
            weave((), lambda k: back_pe(pe, ITEMS - 1, k), SLOTS)


def kernel(**inputs):
    import numpy as np
    import concourse.bacc as bacc
    from concourse import mybir
    from concourse.bass_utils import run_bass_kernel_spmd as run

    a = {k: np.asarray(v) for k, v in inputs.items()}

    def tiles(v):
        return v.reshape(DEPTH, -1, P).transpose(0, 2, 1)

    conv = a["ssm_conv_w"].reshape(DEPTH, 4, 6, P).transpose(0, 3, 1, 2).reshape(DEPTH, P, 24)
    short = a["sc_conv_w"].reshape(DEPTH, 3, 2, P).transpose(0, 3, 1, 2).reshape(DEPTH, P, 6)
    item = np.arange(ITEMS)
    cst = np.stack([item % NB != 0, (item % NB) * P * BIG, (item // NB) * NEXP], -1).astype(np.float32)
    arrays = {
        "x": a["x"].reshape(SEQ, D),
        "w_in": a["w_in"].reshape(DEPTH, KT, P, IN_W).transpose(0, 2, 1, 3),
        "w_out": a["w_out"].reshape(DEPTH * D, D),
        "w_q": a["peer_w_q"].reshape(DEPTH, KT, P, KT, P).transpose(0, 3, 2, 1, 4).reshape(DEPTH * D, D),
        "keys": a["peer_sub_keys"].transpose(0, 3, 1, 2),
        "pk": np.concatenate([conv, tiles(a["ssm_conv_b"]), short, tiles(a["norm1_w"]),
                              tiles(a["ssm_norm_w"])], -1),
        "rows": np.concatenate([a["ssm_dt_bias"], a["ssm_A_log"], a["ssm_D"]], -1),
        "norm2": a["norm2_w"],
        "fnorm": a["final_norm_w"].reshape(1, D),
        "cst": np.broadcast_to(cst, (P, ITEMS, 3)),
        "peer_u": a["peer_u"].reshape(DEPTH * NEXP, D),
        "peer_v": a["peer_v"].reshape(DEPTH * NEXP, D),
    }
    arrays = {f"in_{k}": np.ascontiguousarray(v) for k, v in arrays.items()}
    nc = bacc.Bacc("TRN2", target_bir_lowering=False, num_devices=1)
    args = [nc.dram_tensor(k, v.shape, mybir.dt.from_np(v.dtype), kind="ExternalInput").ap()
            for k, v in arrays.items()]
    stream = nc.dram_tensor("stream", ((ITEMS + NB) * P, D), F32, kind="Internal").ap()
    out = nc.dram_tensor("out", (SEQ, D), F32, kind="ExternalOutput").ap()
    build(nc, *args, stream, out)
    result = run(nc, [arrays], core_ids=[0])
    return result.results[0]["out"].reshape(1, SEQ, D)
```

```python
from contextlib import ExitStack

import concourse.bass as bass
from concourse import mybir

F32 = mybir.dt.float32
U32 = mybir.dt.uint32
ALU = mybir.AluOpType
ACT = mybir.ActivationFunctionType
AX = mybir.AxisListType.X

P = 128
D = 1024
KT = D // P
SEQ, DEPTH = 1024, 2
NB = SEQ // P
ITEMS = NB * DEPTH
IN_W = 2824
Q0, K0, V0, Z0, XBC0, DT0, SB0, SC0, SV0 = 0, 256, 512, 768, 1280, 2048, 2056, 2312, 2568
HD = 64
NH_SB, NH_SSM = 4, 8
NEXP = 16384
TOPK, PH = 16, 4
SLOTS = TOPK * PH
EPS = 1e-6
BIG = 1e30
WS = 2
CHUNKS = 2 * KT
RU, RV, RD = 2, 4, 4
GRP = 8
LAG = 14
NG = SLOTS // GRP
VD = RV - 1
NVD, NVP = SLOTS // RV, SLOTS // RV * (RV - 1)
CW, CB, SCW, SNW, PKW = 0, 24, 30, 36, 40
HB, HS = 8, 4
OB = HB + 5 + HS * 3
QB = OB + 9
EB = OB + 3
EARLY_DVE, EARLY_ACT = 15, 5
DVE_STEPS = 39
ACT_STEPS = 14


def build(nc, x, w_in, w_out, w_q, keys, pk_in, rows_in, norm2, fnorm, norm1, cst_in, peer_u, peer_v, stream, out):
    with ExitStack() as ctx:
        def sb(name, shape, dt=F32):
            return ctx.enter_context(nc.sbuf_tensor(name, shape, dt))

        def ps(name, shape):
            return ctx.enter_context(nc.psum_tensor(name, shape, F32))

        def sem(name):
            return ctx.enter_context(nc.semaphore(name))

        win = sb("win", [P, KT, IN_W])
        wst = sb("wst", [P, WS, D])
        keysT = sb("keysT", [P, 2, P])
        pk = sb("pk", [P, PKW])
        n1 = sb("n1", [P, KT])
        fnrow = sb("fnrow", [P, D])
        rows = sb("rows", [P, 24])
        ident = sb("ident", [P, P])
        tri = sb("tri", [P, P])
        cmr = sb("cmr", [P, SEQ])
        cst = sb("cst", [P, ITEMS, 3])
        iota16 = sb("iota16", [P, TOPK])
        eps = sb("eps", [P, 1])
        kT = sb("kT", [P, 2, SEQ])
        vc = sb("vc", [P, NB, 256])
        state = sb("state", [P, 4, HD])
        pre = sb("pre", [P, 6, 3 + P])
        prod = sb("prod", [P, 2, 2 + P])
        xin = sb("xin", [P, D])
        hT = sb("hT", [P, KT, P])
        hTe = sb("hTe", [P, KT, P])
        qT = sb("qT", [P, 2, P])
        xbcT = sb("xbcT", [P, 6, P])
        cur = sb("cur", [P, 3])
        keep = sb("keep", [P, 1])
        sm = sb("sm", [P, 16])
        dts = sb("dts", [P, 6, 8])
        cd = sb("cd", [P, 8])
        dec = sb("dec", [P, 8])
        negA = sb("negA", [P, 8])
        AR = [sb(f"ar{i}", [P, D]) for i in range(6)]
        cbm = AR[5][:, 0:256].rearrange("p (g l) -> p g l", g=2)
        btok = AR[5][:, 256:384]
        scb = AR[5][:, 768:1024].rearrange("p (c t) -> p c t", c=2)
        zs = AR[4][:, 512:1024]
        y_ssm = AR[5][:, 0:512]
        t8 = sb("t8", [P, 8, TOPK])
        ti = sb("ti", [P, 8, TOPK], U32)
        tf = sb("tf", [P, 8, TOPK])
        bv = sb("bv", [P, PH, TOPK])
        bp = sb("bp", [P, PH, TOPK], U32)
        bab = sb("bab", [P, 2, SLOTS], U32)
        baf = AR[5][:, 0:2 * SLOTS].rearrange("p (t s) -> p t s", t=2)
        eid = sb("eid", [P, 2, SLOTS])
        idxF = sb("idxF", [P, SLOTS], U32)
        gateF = sb("gateF", [P, PH, TOPK])
        gsum = sb("gsum", [P, 2, PH])
        hP = sb("hP", [P, D])
        xP = sb("xP", [P, D])
        idxU = sb("idxU", [P, SLOTS], U32)
        idxV = sb("idxV", [P, SLOTS], U32)
        gateP = sb("gateP", [P, SLOTS])
        dots = sb("dots", [P, SLOTS])
        gel = sb("gel", [P, SLOTS])
        wgt = sb("wgt", [P, SLOTS])
        uring = sb("uring", [P, RU, D])
        vring = sb("vring", [P, RV, D])
        diag = sb("diag", [P, RD, P])
        smP = sb("smP", [P, 4])

        pA = ps("pA", [P, D])
        pB = ps("pB", [P, D])
        pCD = ps("pCD", [P, D])
        pC, pD = pCD[:, 0:512], pCD[:, 512:1024]
        acc = ps("acc", [P, D])

        s_boot = sem("s_boot")
        s_tri = sem("s_tri")
        s_const = sem("s_const")
        s_cst = sem("s_cst")
        s_stream = sem("s_stream")
        s_copy = sem("s_copy")
        s_out = sem("s_out")
        s_par = sem("s_par")
        s_win = [sem(f"s_win{k}") for k in range(KT)]
        s_wst = [sem(f"s_wst{k}") for k in range(WS)]
        s_wused = sem("s_wused")
        s_x = sem("s_x")
        s_hand = sem("s_hand")
        s_idx = sem("s_idx")
        s_handv = sem("s_handv")
        s_dve = sem("s_dve")
        s_act = sem("s_act")
        s_dve_e, s_act_e = sem("s_dve_e"), sem("s_act_e")
        s_xe, s_n1 = sem("s_xe"), sem("s_n1")
        s_n2row, s_keys = sem("s_n2row"), sem("s_keys")
        s_fence = sem("s_fence")
        s_ss1, s_xn, s_hTp, s_hTr = sem("s_ss1"), sem("s_xn"), sem("s_hTp"), sem("s_hTr")
        s_proj = sem("s_proj")
        s_hist, s_qk, s_xbc, s_v, s_ez = sem("s_hist"), sem("s_qk"), sem("s_xbc"), sem("s_v"), sem("s_ez")
        s_cpre, s_cT = sem("s_cpre"), sem("s_cT")
        s_dtr, s_sp, s_a = sem("s_dtr"), sem("s_sp"), sem("s_a")
        s_xtok, s_acs, s_eacs, s_seg, s_L, s_tok = (sem("s_xtok"), sem("s_acs"), sem("s_eacs"), sem("s_seg"),
                                                    sem("s_L"), sem("s_tok"))
        s_G, s_ydg, s_st, s_ys, s_yn, s_ynT = (sem("s_G"), sem("s_ydg"), sem("s_st"), sem("s_ys"),
                                               sem("s_yn"), sem("s_ynT"))
        s_z, s_zm, s_lg, s_cum, s_w, s_wTp, s_wT, s_pv, s_yT = (
            sem("s_z"), sem("s_zm"), sem("s_lg"), sem("s_cum"), sem("s_w"), sem("s_wTp"), sem("s_wT"),
            sem("s_pv"), sem("s_yT"))
        s_ysb = sem("s_ysb")
        s_mix, s_x2, s_xn2, s_h2, s_h2Tp, s_h2T, s_q2T, s_sc = (
            sem("s_mix"), sem("s_x2"), sem("s_xn2"), sem("s_h2"), sem("s_h2Tp"), sem("s_h2T"),
            sem("s_q2T"), sem("s_sc"))
        s_gd, s_ge, s_route, s_keyed = sem("s_gd"), sem("s_ge"), sem("s_route"), sem("s_keyed")
        s_lu = [sem(f"s_lu{k}") for k in range(RU)]
        s_lv = [sem(f"s_lv{k}") for k in range(RV)]
        s_free = sem("s_free")
        s_dot, s_gel, s_wgt, s_diag, s_vused = sem("s_dot"), sem("s_gel"), sem("s_wgt"), sem("s_diag"), sem("s_vused")
        s_vdve = sem("s_vdve")
        s_xo, s_fr, s_fin = sem("s_xo"), sem("s_fr"), sem("s_fin")

        def chain(eng, s, base):
            count = [0]

            def then(ins):
                count[0] += 1
                ins.then_inc(s, 1)
                eng.wait_ge(s, base + count[0])
            return then, count

        def wide(ap, n):
            return ap[:, :, None].to_broadcast((P, ap.shape[1], n))

        def wcols(a, j):
            return win[:, a, j:j + P]

        def load_w_in(sp, layer):
            if layer:
                sp.wait_ge(s_proj, 6 * NB)
                sp.wait_ge(s_hTr, NB)
            sp.dma_start(n1[:, :], norm1[layer]).then_inc(s_n1, 16)
            for k in range(KT):
                sp.dma_start(win[:, k, :], w_in[layer, :, k, :]).then_inc(s_win[k], 16)

        def load_small(sp, layer):
            if layer:
                sp.wait_ge(s_yT, NB)
            sp.dma_start(pk[:, :], pk_in[layer]).then_inc(s_par, 16)
            sp.dma_start(rows[:, :], rows_in[layer:layer + 1, :].to_broadcast((P, 24))).then_inc(s_par, 16)

        def load_keys(sp, layer):
            if layer:
                sp.wait_ge(s_sc, NB)
            sp.dma_start(keysT[:, :, :], keys[layer]).then_inc(s_keys, 16)

        def load_x_residual(sp, m):
            sp.wait_ge(s_vdve, NVD * (m - 1) + 1)
            sp.sem_inc(s_fence, 1)
            sp.dma_start(xin[:, :], stream[bass.ds(m * P, P), :]).then_inc(s_x, 16)

        def load_x_norm(sp, m, layer):
            if layer:
                sp.wait_ge(s_stream, 16 * (m - NB + 1))
                sp.sem_inc(s_fence, 1)
            sp.wait_ge(s_wTp, NH_SB * m - 1)
            sp.sem_inc(s_fence, 1)
            sp.dma_start(AR[0][:, :], stream[bass.ds(m * P, P), :]).then_inc(s_xe, 16)

        def mix_weights(sp, m, first, next_layer):
            if next_layer is not None:
                load_x_norm(sp, m + 1, next_layer)
            for c in range(CHUNKS):
                if c == WS:
                    sp.wait_ge(s_wTp, NH_SB * (m + 1))
                    sp.sem_inc(s_fence, 1)
                    sp.dma_start(AR[1][:, :], norm2[bass.ds(m // NB, 1), :].to_broadcast((P, D))).then_inc(s_n2row, 16)
                if not (first and c < WS):
                    sp.wait_ge(s_wused, m * CHUNKS + c - WS + 1)
                    sp.sem_inc(s_fence, 1)
                if c < KT:
                    src = w_out[bass.ds((m // NB) * D + c * P, P), :]
                else:
                    src = w_q[bass.ds((m // NB) * D + (c - KT) * P, P), :]
                sp.dma_start(wst[:, c % WS, :], src).then_inc(s_wst[c % WS], 16)

        def peer_stores(sp, n):
            sp.wait_ge(s_xo, n + 1)
            sp.sem_inc(s_fence, 1)
            sp.dma_start(stream[bass.ds((n + NB) * P, P), :], xP[:, :]).then_inc(s_stream, 16)
            sp.wait_ge(s_fin, n + 1)
            sp.sem_inc(s_fence, 1)
            sp.dma_start(out[bass.ds((n % NB) * P, P), :], xP[:, :]).then_inc(s_out, 16)

        def root(act, then, col, total, width):
            then(act.activation(sm[:, col:col + 1], total, ACT.Ln, scale=1.0 / width, bias=eps[:, 0:1]))
            then(act.activation(sm[:, col:col + 1], sm[:, col:col + 1], ACT.Exp, scale=-0.5))

        def early_act(act, m, later=True):
            then, count = chain(act, s_act_e, m * EARLY_ACT)
            yield OB - 1
            act.wait_ge(s_xe, 16 * m + 16)
            then(act.activation(AR[2][:, :], AR[0][:, :], ACT.Square, accum_out=sm[:, 0:1]))
            root(act, then, 1, sm[:, 0:1], D)
            act.activation(AR[0][:, :], AR[0][:, :], ACT.Copy, scale=sm[:, 1:2]).then_inc(s_xn, 1)
            yield EB + 4
            act.wait_ge(s_hist, m + 1)
            act.wait_ge(s_proj, 6 * m + 1)
            act.activation(pre[:, 0:4, 3:3 + P], pC[:, :].rearrange("p (c t) -> p c t", c=4),
                           ACT.Copy).then_inc(s_xbc, 1)
            yield EB + 8
            act.wait_ge(s_proj, 6 * m + 2)
            act.activation(pre[:, 4:6, 3:3 + P], pD[:, 0:256].rearrange("p (c t) -> p c t", c=2),
                           ACT.Copy).then_inc(s_xbc, 1)
            act.activation(prod[:, :, 2:2 + P], pD[:, 256:512].rearrange("p (c t) -> p c t", c=2),
                           ACT.Copy).then_inc(s_xbc, 1)
            yield EB + 13
            act.wait_ge(s_cpre, m + 1)
            for i in range(6):
                ins = act.activation(xbcT[:, i, :], AR[5][:, i * P:(i + 1) * P], ACT.Silu,
                                     bias=pk[:, CB + i:CB + i + 1])
            ins.then_inc(s_cT, 1)
            yield EB + 17
            act.wait_ge(s_proj, 6 * m + 3)
            act.activation(qT[:, :, :], pC[:, 0:256].rearrange("p (c t) -> p c t", c=2), ACT.Copy,
                           scale=HD ** -0.5).then_inc(s_qk, 1)
            act.activation(kT[:, :, bass.ds((m % NB) * P, P)], pC[:, 256:512].rearrange("p (c t) -> p c t", c=2),
                           ACT.Copy).then_inc(s_qk, 1)
            yield 53
            act.wait_ge(s_proj, 6 * m + 5)
            act.activation(dts[:, 0, :], pB[:, 256:264], ACT.Copy)
            act.sem_inc(s_fence, 1)
            act.activation(vc[:, bass.ds(m % NB, 1), :].rearrange("p a c -> p (a c)"), pB[:, 0:256],
                           ACT.Copy).then_inc(s_v, 1)
            yield 55
            act.wait_ge(s_dtr, m + 1)
            then(act.activation(dts[:, 1, :], dts[:, 0, :], ACT.Abs))
            then(act.activation(dts[:, 1, :], dts[:, 1, :], ACT.Exp, scale=-1.0))
            act.activation(negA[:, :], rows[:, 8:16], ACT.Exp)
            act.activation(dts[:, 1, :], dts[:, 1, :], ACT.Ln, bias=1.0).then_inc(s_sp, 1)
            yield 58
            if later:
                act.wait_ge(s_gd, m)
            act.wait_ge(s_proj, 6 * m + 6)
            act.activation(zs[:, :], pB[:, 512:1024], ACT.Silu).then_inc(s_ez, 1)
            assert count[0] == EARLY_ACT, count

        def mix_act(act, m, early_next):
            then, count = chain(act, s_act, m * ACT_STEPS)
            yield 1
            act.wait_ge(s_seg, m + 1)
            act.activation(dts[:, 5, :], dts[:, 4, :], ACT.Exp)
            act.activation(cd[:, :], cd[:, :], ACT.Exp).then_inc(s_eacs, 1)
            act.activation(AR[2][:, :], AR[2][:, :], ACT.Exp).then_inc(s_L, 1)
            yield HB - 2
            act.wait_ge(s_ys, m + 1)
            then(act.activation(AR[4][:, 0:512], y_ssm, ACT.Square, accum_out=sm[:, 2:3]))
            root(act, then, 3, sm[:, 2:3], 512)
            act.activation(y_ssm, y_ssm, ACT.Copy, scale=sm[:, 3:4]).then_inc(s_yn, 1)
            def log_part(h):
                zm, lg = AR[h % 2], AR[2 + h % 2]
                act.wait_ge(s_zm, NH_SB * m + h + 1)
                then(act.activation(lg[:, :], zm[:, :], ACT.Abs))
                then(act.activation(lg[:, :], lg[:, :], ACT.Exp, scale=-1.0))
                act.activation(lg[:, :], lg[:, :], ACT.Ln, bias=1.0).then_inc(s_lg, 1)

            yield HB - 1
            log_part(0)
            for h in range(NH_SB):
                yield HB + 1 + HS * h
                act.wait_ge(s_cum, NH_SB * m + h + 1)
                act.activation(AR[h % 2][:, :], AR[h % 2][:, :], ACT.Exp).then_inc(s_w, 1)
                yield HB + 3 + HS * h
                act.wait_ge(s_wTp, NH_SB * m + h + 1)
                act.activation(AR[5][:, :], pB[:, :], ACT.Copy).then_inc(s_wT, 1)
                if h + 1 < NH_SB:
                    log_part(h + 1)
            yield OB - 1
            act.wait_ge(s_pv, NH_SB * (m + 1))
            act.activation(hT[:, 0:2, :], pC[:, 0:256].rearrange("p (c t) -> p c t", c=2),
                           ACT.Copy).then_inc(s_ysb, 1)
            yield QB - 3
            act.wait_ge(s_x2, m + 1)
            if early_next:
                act.wait_ge(s_hTp, m + 2)
            then(act.activation(AR[0][:, :], xin[:, :], ACT.Square, accum_out=sm[:, 4:5]))
            root(act, then, 5, sm[:, 4:5], D)
            act.activation(AR[0][:, :], xin[:, :], ACT.Copy, scale=sm[:, 5:6]).then_inc(s_xn2, 1)
            yield QB - 1
            act.wait_ge(s_h2Tp, m + 1)
            act.activation(hT[:, :, :], pB[:, :].rearrange("p (c t) -> p c t", c=KT), ACT.Copy).then_inc(s_h2T, 1)
            yield QB + 7
            act.wait_ge(s_wused, CHUNKS * m + CHUNKS)
            act.activation(AR[2][:, :], pA[:, :], ACT.Copy).then_inc(s_q2T, 1)
            yield 55
            act.wait_ge(s_gd, m + 1)
            act.activation(gateF[:, :, :], gateF[:, :, :], ACT.Exp).then_inc(s_ge, 1)
            assert count[0] == ACT_STEPS, count

        def early_pe(pe, m, later=True):
            yield OB + 1
            pe.wait_ge(s_xn, m + 1)
            for k in range(KT):
                mm = pe.transpose(pCD[:, k * P:(k + 1) * P], AR[0][:, k * P:(k + 1) * P], ident[:, :])
            mm.then_inc(s_hTp, 1)
            yield EB
            pe.wait_ge(s_hTr, m + 1)
            for k in range(KT):
                pe.wait_ge(s_win[k], 16 * (m // NB) + 16)
            banks = ((pC, [XBC0 + P * i for i in range(4)]),
                     (pD, [XBC0 + 4 * P, XBC0 + 5 * P, SC0, SC0 + P]),
                     (pC, [Q0, Q0 + P, K0, K0 + P]),
                     (pD, [SB0, SB0 + P, SV0, SV0 + P]))
            for b, (bank, cols) in enumerate(banks):
                for i, c0 in enumerate(cols):
                    yield EB + 4 * b + i + (5 if b >= 2 else 0)
                    if b == 2 and i == 0:
                        pe.wait_ge(s_xbc, 3 * m + 1)
                    if b == 3 and i == 0:
                        pe.wait_ge(s_xbc, 3 * m + 3)
                    for k in range(KT):
                        mm = pe.matmul(bank[:, i * P:(i + 1) * P], wcols(k, c0), hTe[:, k, :],
                                       start=(k == 0), stop=(k == KT - 1))
                mm.then_inc(s_proj, 1)
            for i, (c0, width, at) in enumerate(((V0, 256, 0), (DT0, 8, 256), (Z0, 256, 512), (Z0 + 256, 256, 768))):
                yield 50 + 2 * i
                if later and i == 0:
                    pe.wait_ge(s_keyed, m)
                for k in range(KT):
                    mm = pe.matmul(pB[:, at:at + width], hTe[:, k, :], win[:, k, c0:c0 + width],
                                   start=(k == 0), stop=(k == KT - 1))
                if c0 in (DT0, Z0 + 256):
                    mm.then_inc(s_proj, 1)

        def mix_pe(pe, m):
            yield 0
            pe.wait_ge(s_a, m + 1)
            pe.wait_ge(s_v, m + 1)
            pe.wait_ge(s_ez, m + 1)
            pe.wait_ge(s_xbc, 3 * m + 3)
            pe.matmul(pD[:, 384:392], tri[:, :], dts[:, 3, :], start=True, stop=True)
            for h in range(NH_SSM):
                mm = pe.matmul(pA[:, h * P:(h + 1) * P], dts[:, 3, h:h + 1].to_broadcast((P, P)), tri[:, :],
                               start=True, stop=True)
            mm.then_inc(s_acs, 1)
            yield 1
            pe.wait_ge(s_cT, m + 1)
            pe.wait_ge(s_seg, m + 1)
            pe.wait_ge(s_qk, 2 * m + 2)
            for i in range(4):
                pe.transpose(pC[:, i * P:(i + 1) * P], xbcT[:, i, :], ident[:, :])
            pe.transpose(pD[:, 0:P], xbcT[:, 4, :], ident[:, :])
            for g in range(2):
                lo = g * HD
                mm = pe.matmul((pD, pA)[g][:, P:2 * P], xbcT[lo:lo + HD, 4, :], xbcT[lo:lo + HD, 5, :],
                               start=True, stop=True)
            mm.then_inc(s_xtok, 1)
            yield 3
            pe.wait_ge(s_tok, m + 1)
            for g in range(2):
                lo = g * HD
                pe.matmul((pB, pA)[g][:, 512:768], xbcT[lo:lo + HD, 5, :],
                          state[lo:lo + HD, :, :].rearrange("p h d -> p (h d)"), start=True, stop=True)
            pe.matmul(pC[:, :], btok[:, :], AR[4][:, 0:512], start=True, stop=True).then_inc(s_ydg, 1)
            yield 3
            pe.wait_ge(s_G, m + 1)
            for h in range(NH_SSM):
                mm = pe.matmul(pB[:, h * HD:(h + 1) * HD], AR[2][:, h * P:(h + 1) * P],
                               AR[3][:, h * HD:(h + 1) * HD], start=True, stop=True)
            mm.then_inc(s_ydg, 1)
            def scores(h):
                c, lo = h // 2, HD * (h % 2)
                for j in range(2):
                    mm = pe.matmul(pA[:, j * 512:(j + 1) * 512], qT[lo:lo + HD, c, :],
                                   kT[lo:lo + HD, c, j * 512:(j + 1) * 512], start=True, stop=True)
                mm.then_inc(s_z, 1)
            yield 5
            pe.wait_ge(s_st, m + 1)
            scores(0)
            yield HB
            pe.wait_ge(s_yn, m + 1)
            for i in range(4):
                mm = pe.transpose(pD[:, i * P:(i + 1) * P], y_ssm[:, i * P:(i + 1) * P], ident[:, :])
            mm.then_inc(s_ynT, 1)
            for h in range(NH_SB):
                c, lo = h // 2, HD * (h % 2)
                if h + 1 < NH_SB:
                    yield HB + HS * h
                    pe.wait_ge(s_zm, NH_SB * m + h + 1)
                    scores(h + 1)
                yield HB + 2 + HS * h
                pe.wait_ge(s_w, NH_SB * m + h + 1)
                for j in range(NB):
                    mm = pe.transpose(pB[:, j * P:(j + 1) * P], AR[h % 2][:, j * P:(j + 1) * P], ident[:, :])
                mm.then_inc(s_wTp, 1)
                yield HB + 4 + HS * h
                pe.wait_ge(s_wT, NH_SB * m + h + 1)
                for j in range(NB):
                    mm = pe.matmul(pC[lo:lo + HD, c * P:(c + 1) * P], vc[:, j, h * HD:(h + 1) * HD],
                                   AR[5][:, j * P:(j + 1) * P], start=(j == 0), stop=(j == NB - 1))
                mm.then_inc(s_pv, 1)
            yield OB
            pe.wait_ge(s_ysb, m + 1)
            pe.wait_ge(s_yT, m + 1)
            for c in range(KT):
                yield OB + c * 7 // 8
                pe.wait_ge(s_wst[c % WS], 16 * (m * (CHUNKS // WS) + c // WS + 1))
                for j in range(2):
                    mm = pe.matmul(pA[:, j * 512:(j + 1) * 512], hT[:, c, :],
                                   wst[:, c % WS, j * 512:(j + 1) * 512], start=(c == 0), stop=(c == KT - 1))
                mm.then_inc(s_wused, 1)
            yield QB - 1
            pe.wait_ge(s_h2, m + 1)
            for k in range(KT):
                mm = pe.transpose(pB[:, k * P:(k + 1) * P], AR[1][:, k * P:(k + 1) * P], ident[:, :])
            mm.then_inc(s_h2Tp, 1)
            pe.wait_ge(s_h2T, m + 1)
            for j in range(KT):
                c = KT + j
                yield QB + j * 7 // 8
                pe.wait_ge(s_wst[c % WS], 16 * (m * (CHUNKS // WS) + c // WS + 1))
                for k in range(KT):
                    mm = pe.matmul(pA[:, j * P:(j + 1) * P], wst[:, c % WS, k * P:(k + 1) * P], hT[:, k, :],
                                   start=(k == 0), stop=(k == KT - 1))
                mm.then_inc(s_wused, 1)
            yield QB + 7
            pe.wait_ge(s_q2T, m + 1)
            pe.wait_ge(s_keys, 16 * (m // NB) + 16)
            for j in range(KT):
                mm = pe.matmul(pB[:, j * P:(j + 1) * P], AR[2][:, j * P:(j + 1) * P], keysT[:, j % 2, :],
                               start=True, stop=True)
            mm.then_inc(s_sc, 1)

        def early_dve(dve, m):
            then, count = chain(dve, s_dve_e, m * EARLY_DVE)
            tt, ts, stt = dve.tensor_tensor, dve.tensor_scalar, dve.scalar_tensor_tensor
            yield OB + 1
            then(ts(keep[:, :], cst[:, bass.ds(m, 1), 0], 1.0, None, ALU.mult))
            ts(state[:, :, :], state[:, :, :], keep[:, 0:1], None, ALU.mult)
            ts(prod[:, :, 0:2], prod[:, :, P:P + 2], keep[:, 0:1], None, ALU.mult)
            ts(pre[:, :, 0:3], pre[:, :, P:P + 3], keep[:, 0:1], None, ALU.mult).then_inc(s_hist, 1)
            yield OB + 2
            dve.wait_ge(s_n1, 16 * (m // NB) + 16)
            dve.wait_ge(s_hTp, m + 1)
            tt(hTe[:, :, :], pCD[:, :].rearrange("p (c t) -> p c t", c=KT), wide(n1[:, :], P),
               ALU.mult).then_inc(s_hTr, 1)
            c0 = AR[5][:, 0:768].rearrange("p (c t) -> p c t", c=6)
            c1 = AR[4][:, 0:768].rearrange("p (c t) -> p c t", c=6)
            cw = pk[:, CW:CW + 24].rearrange("p (j c) -> p j c", j=4)
            yield EB + 9
            dve.wait_ge(s_par, 32 * (m // NB) + 32)
            dve.wait_ge(s_xbc, 3 * m + 3)
            then(tt(c0, pre[:, :, 0:P], wide(cw[:, 0, :], P), ALU.mult))
            for j in range(1, 4):
                yield EB + 9 + j
                ins = tt(c1, pre[:, :, j:j + P], wide(cw[:, j, :], P), ALU.mult)
                then(ins)
                ins = tt(c0, c0, c1, ALU.add)
                if j < 3:
                    then(ins)
            ins.then_inc(s_cpre, 1)
            dve.wait_ge(s_cpre, m + 1)
            yield 53
            dve.wait_ge(s_proj, 6 * m + 4)
            dve.tensor_copy(scb[:, :, :], pD[:, 0:256].rearrange("p (c t) -> p c t", c=2))
            then(tt(prod[:, :, 2:2 + P], prod[:, :, 2:2 + P], pD[:, 256:512].rearrange("p (c t) -> p c t", c=2),
                    ALU.mult))
            s0 = AR[4][:, 0:256].rearrange("p (c t) -> p c t", c=2)
            s1 = AR[4][:, 256:512].rearrange("p (c t) -> p c t", c=2)
            sw = pk[:, SCW:SCW + 6].rearrange("p (j c) -> p j c", j=3)
            then(tt(s0, prod[:, :, 0:P], wide(sw[:, 0, :], P), ALU.mult))
            for j in range(1, 3):
                then(tt(s1, prod[:, :, j:j + P], wide(sw[:, j, :], P), ALU.mult))
                then(tt(s0, s0, s1, ALU.add))
            then(tt(hT[:, 6:8, :], s0, scb[:, :, :], ALU.mult))
            yield 55
            dve.wait_ge(s_v, m + 1)
            tt(dts[:, 0, :], dts[:, 0, :], rows[:, 0:8], ALU.add).then_inc(s_dtr, 1)
            yield 58
            dve.wait_ge(s_sp, m + 1)
            then(stt(out=dts[:, 2, :], in0=dts[:, 0, :], scalar=0.0, in1=dts[:, 1, :], op0=ALU.max, op1=ALU.add))
            stt(out=dts[:, 3, :], in0=dts[:, 2, :], scalar=-1.0, in1=negA[:, :], op0=ALU.mult,
                op1=ALU.mult).then_inc(s_a, 1)
            assert count[0] == EARLY_DVE, count

        def mix_dve(dve, m, early_next):
            then, count = chain(dve, s_dve, m * DVE_STEPS)
            tt, ts, stt = dve.tensor_tensor, dve.tensor_scalar, dve.scalar_tensor_tensor

            then(ts(cur[:, :], cst[:, bass.ds(m, 1), :].rearrange("p a c -> p (a c)"), 1.0, None, ALU.mult))
            qoff, first_expert = cur[:, 1:2], cur[:, 2:3]
            yield 1
            dve.wait_ge(s_acs, m + 1)
            dve.tensor_copy(cd[:, :], pA[:, P - 1:D:P])
            then(dve.tensor_copy(dts[:, 4, :], pD[:, 384:392]))
            L = AR[2][:, :].rearrange("p (h l) -> p h l", h=NH_SSM)
            then(tt(L, pA[:, :].rearrange("p (h l) -> p h l", h=NH_SSM), wide(dts[:, 4, :], P), ALU.subtract))
            ts(AR[2][:, :], AR[2][:, :], 0.0, None, ALU.min).then_inc(s_seg, 1)
            yield 3
            xt, xd, xdd = AR[3][:, 512:1024], AR[3][:, 0:512], AR[4][:, 0:512]
            h8 = lambda ap: ap.rearrange("p (h d) -> p h d", h=NH_SSM)
            dve.wait_ge(s_xtok, m + 1)
            dve.tensor_copy(btok[:, :], pD[:, 0:P])
            for g in range(2):
                tt(cbm[:, g, :], (pD, pA)[g][:, P:2 * P], tri[:, :], ALU.mult)
            then(dve.tensor_copy(xt, pC[:, :]))
            then(tt(h8(xd), h8(xt), wide(dts[:, 2, :], HD), ALU.mult))
            dve.wait_ge(s_L, m + 1)
            then(dve.tensor_copy(dec[:, :], AR[2][:, P - 1:D:P]))
            tt(h8(xdd), h8(xd), wide(dec[:, :], HD), ALU.mult).then_inc(s_tok, 1)
            for g in range(2):
                half = L[:, 4 * g:4 * g + 4, :]
                ins = tt(half, half, cbm[:, g:g + 1, :].to_broadcast((P, 4, P)), ALU.mult)
            ins.then_inc(s_G, 1)
            yield 5
            y = y_ssm
            tmp = AR[0][:, 0:512]
            dve.wait_ge(s_ydg, 2 * m + 1)
            dve.wait_ge(s_eacs, m + 1)
            dve.wait_ge(s_G, m + 1)
            for g in range(2):
                lo = g * HD
                tt(state[lo:lo + HD, :, :], state[lo:lo + HD, :, :],
                   cd[lo:lo + HD, 4 * g:4 * g + 4, None].to_broadcast((HD, 4, HD)), ALU.mult)
            for g in range(2):
                ins = tt(h8(y)[:, 4 * g:4 * g + 4, :], (pB, pA)[g][:, 512:768].rearrange("p (h d) -> p h d", h=4),
                         wide(dts[:, 5, 4 * g:4 * g + 4], HD), ALU.mult)
            then(ins)
            for g in range(2):
                lo = g * HD
                ins = tt(state[lo:lo + HD, :, :], state[lo:lo + HD, :, :],
                         pC[lo:lo + HD, 256 * g:256 * g + 256].rearrange("p (h d) -> p h d", h=4), ALU.add)
            ins.then_inc(s_st, 1)
            then(tt(h8(tmp), h8(xt), wide(rows[:, 16:24], HD), ALU.mult))
            then(tt(y, y, tmp, ALU.add))
            yield 6
            dve.wait_ge(s_ydg, 2 * m + 2)
            then(tt(y, y, pB[:, 0:512], ALU.add))
            tt(y, y, zs[:, :], ALU.mult).then_inc(s_ys, 1)
            def masked(h):
                dve.wait_ge(s_z, NH_SB * m + h + 1)
                if h >= 2:
                    dve.wait_ge(s_wTp, NH_SB * m + h - 1)
                stt(out=AR[h % 2][:, :], in0=cmr[:, :], scalar=qoff, in1=pA[:, :], op0=ALU.add,
                    op1=ALU.min).then_inc(s_zm, 1)

            yield HB - 1
            masked(0)
            yield HB + 1
            dve.wait_ge(s_ynT, m + 1)
            tt(hT[:, 2:6, :], pD[:, :].rearrange("p (c t) -> p c t", c=4), wide(pk[:, SNW:SNW + 4], P),
               ALU.mult).then_inc(s_yT, 1)
            for h in range(NH_SB):
                zm, lg, cum = AR[h % 2], AR[2 + h % 2], AR[4]
                yield HB + 1 + HS * h
                dve.wait_ge(s_lg, NH_SB * m + h + 1)
                then(stt(out=lg[:, :], in0=zm[:, :], scalar=0.0, in1=lg[:, :], op0=ALU.max, op1=ALU.add))
                then(dve.tensor_tensor_scan(cum[:, ::-1], lg[:, ::-1], lg[:, ::-1], 0.0, ALU.add, ALU.bypass))
                tt(zm[:, :], zm[:, :], cum[:, :], ALU.subtract).then_inc(s_cum, 1)
                if h + 1 < NH_SB:
                    yield HB + 3 + HS * h
                    masked(h + 1)
            yield QB - 2
            dve.wait_ge(s_wused, CHUNKS * m + KT)
            tt(xin[:, :], xin[:, :], pA[:, :], ALU.add).then_inc(s_x2, 1)
            yield QB
            dve.wait_ge(s_xn2, m + 1)
            dve.wait_ge(s_n2row, 16 * m + 16)
            tt(AR[1][:, :], AR[0][:, :], AR[1][:, :], ALU.mult).then_inc(s_h2, 1)
            yield QB + 9
            dve.wait_ge(s_sc, m + 1)
            dve.sem_inc(s_fence, 1)
            pl = [pB[:, j * P:(j + 1) * P] for j in range(8)]
            wk = [AR[3][:, j * P:(j + 1) * P] for j in range(8)]
            yield from top16(QB + 9, dve, then, pl, wk, [t8[:, j, :] for j in range(8)], [ti[:, j, :] for j in range(8)],
                             s_keyed)
            then(dve.tensor_copy(tf[:, :, :], ti[:, :, :]))
            ht = t8[:, :, :].rearrange("p (h t) k -> p h t k", t=2)
            cand = AR[4][:, :].rearrange("p (h i j) -> p h i j", h=PH, i=TOPK)
            sq = (P, PH, TOPK, TOPK)
            for h in range(PH):
                ins = tt(cand[:, h, :, :], t8[:, 2 * h, :, None].to_broadcast((P, TOPK, TOPK)),
                         t8[:, 2 * h + 1, None, :].to_broadcast((P, TOPK, TOPK)), ALU.add)
            then(ins)
            if early_next:
                dve.wait_ge(s_cT, m + 2)
            dve.sem_inc(s_fence, 1)
            n2 = TOPK * TOPK
            yield from top16(49, dve, then, [AR[4][:, h * n2:(h + 1) * n2] for h in range(PH)],
                  [AR[5][:, h * n2:(h + 1) * n2] for h in range(PH)],
                  [bv[:, h, :] for h in range(PH)], [bp[:, h, :] for h in range(PH)])
            yield 54
            tt(gateF[:, :, :], bv[:, :, :], bv[:, :, 0:1].to_broadcast((P, PH, TOPK)), ALU.subtract).then_inc(s_gd, 1)
            bpf = bp[:, :, :].rearrange("p h k -> p (h k)")
            ts(bab[:, 0, :], bpf, 4, None, ALU.logical_shift_right)
            then(ts(bab[:, 1, :], bpf, 15, None, ALU.bitwise_and))
            then(dve.tensor_copy(baf[:, :, :], bab[:, :, :]))
            hot = AR[3][:, :].rearrange("p (s i) -> p s i", s=SLOTS)
            for t in range(2):
                yield 56 + 2 * t
                then(tt(hot, wide(baf[:, t, :], TOPK), iota16[:, None, :].to_broadcast((P, SLOTS, TOPK)),
                        ALU.is_equal))
                for h in range(PH):
                    part = hot[:, h * TOPK:(h + 1) * TOPK, :]
                    ins = tt(part, part, tf[:, 2 * h + t, None, :].to_broadcast((P, TOPK, TOPK)), ALU.mult)
                then(ins)
                then(dve.tensor_reduce(eid[:, t, :], hot, AX, ALU.add))
            then(stt(out=eid[:, 0, :], in0=eid[:, 0, :], scalar=float(P), in1=eid[:, 1, :], op0=ALU.mult, op1=ALU.add))
            ts(idxF[:, :], eid[:, 0, :], first_expert, None, ALU.add).then_inc(s_idx, 1)
            yield 62
            dve.wait_ge(s_ge, m + 1)
            then(dve.tensor_reduce(gsum[:, 0, :], gateF[:, :, :], AX, ALU.add))
            then(dve.reciprocal(gsum[:, 1, :], gsum[:, 0, :]))
            tt(gateF[:, :, :], gateF[:, :, :], wide(gsum[:, 1, :], TOPK), ALU.mult).then_inc(s_route, 1)
            assert count[0] == DVE_STEPS, count

        def top16(row, dve, then, src, work, vals, idxs, read=None):
            def fenced(ins):
                then(ins)
                dve.sem_inc(s_fence, 1)
            for s, v in zip(src, vals):
                ins = dve.max(v[:, 0:8], s)
            fenced(ins)
            yield row + 1
            for s, w, v, i in zip(src, work, vals, idxs):
                dve.max_index(i[:, 0:8], v[:, 0:8], s)
                ins = dve.match_replace(w, v[:, 0:8], s, -3.0e38)
            fenced(ins)
            if read is not None:
                dve.sem_inc(read, 1)
            yield row + 2
            for w, v in zip(work, vals):
                ins = dve.max(v[:, 8:16], w)
            fenced(ins)
            yield row + 3
            for w, v, i in zip(work, vals, idxs):
                ins = dve.max_index(i[:, 8:16], v[:, 8:16], w)
            then(ins)

        def pe_rows(k):
            return k // RV * (RV - 1) + k % RV

        def gather(pool, ring, slot, table, idx, k, landed):
            pool.indirect_dma_start(ring[:, slot, :], None, table[:, :],
                                    bass.IndirectOffsetOnAxis(idx[:, k:k + 1], 0)).then_inc(landed[slot], 16)

        def both(first, n, k, step, *more):
            if not first:
                step(n - 1, k + SLOTS, *more)
            step(n, k, *more)

        def gather_u(pool, n, k, first):
            if not (first and k < RU):
                pool.wait_ge(s_dot, SLOTS * n + k - RU + 1)
                pool.sem_inc(s_free, 1)
            gather(pool, uring, k % RU, peer_u, idxF if k < 2 * RU else idxU, k, s_lu)

        def gather_v(pool, n, step, first):
            k = step - LAG
            if not 0 <= k < SLOTS:
                return
            if k == 0:
                pool.wait_ge(s_handv, 2 * n + 1)
                pool.sem_inc(s_free, 1)
            if not (first and k < RV):
                if k % RV == VD:
                    pool.wait_ge(s_vdve, NVD * n + k // RV)
                else:
                    pool.wait_ge(s_vused, NVP * n + pe_rows(k - RV) + 1)
                pool.sem_inc(s_free, 1)
            gather(pool, vring, k % RV, peer_v, idxV, k, s_lv)

        def peer_pool(pool, n, first):
            for k in range(SLOTS):
                if k == 0:
                    pool.wait_ge(s_idx, n + 1)
                    pool.sem_inc(s_free, 1)
                if k == 2 * RU:
                    pool.wait_ge(s_hand, n + 1)
                    pool.sem_inc(s_free, 1)
                gather_u(pool, n, k, first)
                both(first, n, k, lambda i, step: gather_v(pool, i, step, first))

        def hand_over(dve, n, first):
            dve.wait_ge(s_route, n + 1)
            if not first:
                dve.wait_ge(s_dot, SLOTS * n)
                dve.wait_ge(s_handv, 2 * n)
            dve.tensor_copy(idxU[:, :], idxF[:, :])
            dve.tensor_copy(hP[:, :], AR[1][:, :]).then_inc(s_hand, 1)
            dve.wait_ge(s_hand, n + 1)

        def v_landed(eng, n, k):
            eng.wait_ge(s_lv[k % RV], 16 * (n * (SLOTS // RV) + k // RV + 1))

        def weights_dve(dve, n, g):
            s = slice(GRP * g, GRP * (g + 1))
            if g == 0:
                dve.wait_ge(s_handv, 2 * n + 1)
            dve.wait_ge(s_gel, NG * n + g + 1)
            dve.tensor_tensor(wgt[:, s], gel[:, s], gateP[:, s], ALU.mult).then_inc(s_wgt, 1)

        def v_dve(dve, n, step, outputs):
            g, v = step - GRP - 2, step - LAG - 1
            if g % GRP == 0 and 0 <= g < SLOTS:
                weights_dve(dve, n, g // GRP)
            if v % RV == VD and 0 <= v < SLOTS:
                v_landed(dve, n, v)
                dve.wait_ge(s_wgt, NG * n + v // GRP + 1)
                if v >= RV:
                    dve.wait_ge(s_vdve, NVD * n + v // RV)
                elif outputs:
                    dve.wait_ge(s_out, 16 * n)
                x_in = xin if v < RV else xP
                dve.scalar_tensor_tensor(out=xP[:, :], in0=vring[:, VD, :], scalar=wgt[:, v:v + 1], in1=x_in[:, :],
                                         op0=ALU.mult, op1=ALU.add).then_inc(s_vdve, 1)

        def back_dve(dve, n, k, first):
            dve.wait_ge(s_lu[k % RU], 16 * (n * (SLOTS // RU) + k // RU + 1))
            u = uring[:, k % RU, :]
            dve.tensor_tensor_reduce(u, u, hP[:, :], 1.0, 0.0, ALU.mult, ALU.add,
                                     dots[:, k:k + 1]).then_inc(s_dot, 1)
            both(first, n, k, lambda i, step: v_dve(dve, i, step, not first))
            if k == LAG - 5:
                if not first:
                    dve.wait_ge(s_wgt, NG * n)
                    dve.wait_ge(s_vused, NVP * n - NVP // NG)
                    dve.wait_ge(s_vdve, NVD * n - NVD // NG)
                dve.tensor_copy(gateP[:, :], gateF[:, :, :].rearrange("p h k -> p (h k)"))
                dve.tensor_copy(idxV[:, 0:SLOTS - GRP], idxU[:, 0:SLOTS - GRP]).then_inc(s_handv, 1)
            if k == LAG:
                if not first:
                    finish_dve(dve, n - 1)
                dve.tensor_copy(idxV[:, SLOTS - GRP:SLOTS], idxU[:, SLOTS - GRP:SLOTS]).then_inc(s_handv, 1)
            if k == LAG + 2 and not first:
                norm_dve(dve, n - 1)

        def v_act(act, n, step, first):
            g, k = step - GRP - 1, step - LAG + 2
            if g % GRP == 0 and 0 <= g < SLOTS:
                s = slice(g, g + GRP)
                act.wait_ge(s_dot, SLOTS * n + g + GRP)
                act.activation(gel[:, s], dots[:, s], ACT.Gelu).then_inc(s_gel, 1)
            if k % RV != VD and 0 <= k < SLOTS:
                r = pe_rows(k)
                act.wait_ge(s_wgt, NG * n + k // GRP + 1)
                if not (first and r < RD):
                    act.wait_ge(s_vused, NVP * n + r - RD + 1)
                act.activation(diag[:, r % RD, :], ident[:, :], ACT.Copy, scale=wgt[:, k:k + 1]).then_inc(s_diag, 1)

        def back_act(act, n, k, first):
            both(first, n, k, lambda i, step: v_act(act, i, step, first))
            if k == LAG and not first:
                finish_act(act, n - 1)

        def v_pe(pe, n, step, outputs):
            k = step - LAG
            if k % RV != VD and 0 <= k < SLOTS:
                r = pe_rows(k)
                if r == 0 and outputs:
                    pe.wait_ge(s_xo, n)
                pe.wait_ge(s_diag, NVP * n + r + 1)
                v_landed(pe, n, k)
                for j in range(2):
                    mm = pe.matmul(acc[:, j * 512:(j + 1) * 512], diag[:, r % RD, :],
                                   vring[:, k % RV, j * 512:(j + 1) * 512], start=(r == 0), stop=(r == NVP - 1))
                mm.then_inc(s_vused, 1)

        def back_pe(pe, n, k, first):
            both(first, n, k, lambda i, step: v_pe(pe, i, step, not first))

        def finish_dve(dve, n):
            dve.wait_ge(s_vused, NVP * (n + 1))
            dve.wait_ge(s_vdve, NVD * (n + 1))
            dve.tensor_tensor(xP[:, :], xP[:, :], acc[:, :], ALU.add).then_inc(s_xo, 1)
            dve.wait_ge(s_xo, n + 1)

        def norm_dve(dve, n):
            dve.wait_ge(s_fr, 3 * n + 3)
            dve.wait_ge(s_stream, 16 * n + 16)
            dve.scalar_tensor_tensor(out=xP[:, :], in0=xP[:, :], scalar=smP[:, 1:2], in1=fnrow[:, :],
                                     op0=ALU.mult, op1=ALU.mult).then_inc(s_fin, 1)

        def finish_act(act, n):
            act.wait_ge(s_xo, n + 1)
            act.activation(hTe[:, :, :].rearrange("p c t -> p (c t)"), xP[:, :], ACT.Square, accum_out=smP[:, 0:1]).then_inc(s_fr, 1)
            act.wait_ge(s_fr, 3 * n + 1)
            act.activation(smP[:, 1:2], smP[:, 0:1], ACT.Ln, scale=1.0 / D, bias=eps[:, 0:1]).then_inc(s_fr, 1)
            act.wait_ge(s_fr, 3 * n + 2)
            act.activation(smP[:, 1:2], smP[:, 1:2], ACT.Exp, scale=-0.5).then_inc(s_fr, 1)

        def alone(front):
            for _ in front:
                pass

        def merge(front, early):
            parts = [iter(front), iter(early)]
            rows = [next(part, None) for part in parts]
            while any(row is not None for row in rows):
                i = min((i for i in range(2) if rows[i] is not None), key=lambda i: (rows[i], i))
                yield rows[i]
                rows[i] = next(parts[i], None)

        def weave(front, back, rows):
            k = 0
            for row in front:
                assert row <= rows
                while k < row:
                    back(k)
                    k += 1
            while k < rows:
                back(k)
                k += 1

        block = ctx.enter_context(nc.Block())

        @block.sync
        def _(sp):
            sp.dma_start(AR[0][:, :], x[0:P, :]).then_inc(s_xe, 16)
            load_w_in(sp, 0)
            sp.dma_start(xin[:, :], x[0:P, :]).then_inc(s_x, 16)
            sp.dma_start(cst[:, :, :], cst_in[:, :, :]).then_inc(s_cst, 16)
            load_small(sp, 0)
            load_keys(sp, 0)
            sp.dma_start(fnrow[:, :], fnorm[0:1, :].to_broadcast((P, D))).then_inc(s_cst, 16)
            sp.dma_start(stream[0:SEQ, :], x[:, :]).then_inc(s_copy, 16)
            sp.wait_ge(s_copy, 16)
            mix_weights(sp, 0, True, 0)

            def item(n, next_layer, outputs=True, small=False):
                if outputs:
                    peer_stores(sp, n - 1)
                load_x_residual(sp, n + 1)
                if small:
                    load_small(sp, 1)
                mix_weights(sp, n + 1, False, next_layer)
            item(0, 0, False)
            with sp.Fori(1, NB - 2) as n:
                item(n, 0)
            load_w_in(sp, 1)
            item(NB - 2, 1, True, True)
            load_keys(sp, 1)
            with sp.Fori(NB - 1, ITEMS - 2) as n:
                item(n, 1)
            item(ITEMS - 2, None)
            peer_stores(sp, ITEMS - 2)
            peer_stores(sp, ITEMS - 1)
            sp.wait_ge(s_stream, 16 * ITEMS)
            sp.wait_ge(s_out, 16 * ITEMS)

        @block.gpsimd
        def _(pool):
            pool.memset(ident[:, :], 0.0)
            pool.memset(tri[:, :], 1.0)
            pool.memset(kT[:, :, :], 0.0)
            pool.memset(vc[:, :, :], 0.0)
            pool.memset(state[:, :, :], 0.0)
            pool.memset(pre[:, :, :], 0.0)
            pool.memset(prod[:, :, :], 0.0)
            pool.memset(eps[:, :], EPS)
            pool.iota(iota16[:, :], [[1, TOPK]], base=0, channel_multiplier=0,
                      allow_small_or_imprecise_dtypes=True)
            pool.iota(cmr[:, :], [[-1, SEQ]], base=0, channel_multiplier=1,
                      allow_small_or_imprecise_dtypes=True).then_inc(s_tri, 1)
            pool.wait_ge(s_tri, 1)
            pool.affine_select(out=ident[:, :], in_=ident[:, :], compare_op=ALU.not_equal, fill=1.0,
                               base=0, pattern=[[-1, P]], channel_multiplier=1)
            pool.affine_select(out=tri[:, :], in_=tri[:, :], compare_op=ALU.is_ge, fill=0.0,
                               base=0, pattern=[[1, P]], channel_multiplier=-1).then_inc(s_boot, 6)
            peer_pool(pool, 0, True)
            with pool.Fori(1, ITEMS) as n:
                peer_pool(pool, n, False)
            for k in range(LAG):
                gather_v(pool, ITEMS - 1, SLOTS + k, False)

        @block.vector
        def _(dve):
            dve.wait_ge(s_boot, 6)
            dve.tensor_scalar(cmr[:, :], cmr[:, :], -0.5, BIG, ALU.add, ALU.mult).then_inc(s_const, 1)
            dve.wait_ge(s_const, 1)
            dve.wait_ge(s_cst, 32)

            def item(n, front, first=False):
                hand_over(dve, n, first)
                weave(front, lambda k: back_dve(dve, n, k, first), SLOTS)
            alone(early_dve(dve, 0))
            alone(merge(mix_dve(dve, 0, True), early_dve(dve, 1)))
            item(0, merge(mix_dve(dve, 1, True), early_dve(dve, 2)), True)
            with dve.Fori(1, ITEMS - 2) as n:
                item(n, merge(mix_dve(dve, n + 1, True), early_dve(dve, n + 2)))
            item(ITEMS - 2, mix_dve(dve, ITEMS - 1, False))
            item(ITEMS - 1, ())
            for k in range(LAG + 1):
                v_dve(dve, ITEMS - 1, SLOTS + k, True)
            finish_dve(dve, ITEMS - 1)
            norm_dve(dve, ITEMS - 1)

        @block.scalar
        def _(act):
            def item(n, front, first=False):
                weave(front, lambda k: back_act(act, n, k, first), SLOTS)
            act.wait_ge(s_boot, 6)
            alone(early_act(act, 0, False))
            alone(merge(mix_act(act, 0, True), early_act(act, 1)))
            item(0, merge(mix_act(act, 1, True), early_act(act, 2)), True)
            with act.Fori(1, ITEMS - 2) as n:
                item(n, merge(mix_act(act, n + 1, True), early_act(act, n + 2)))
            item(ITEMS - 2, mix_act(act, ITEMS - 1, False))
            item(ITEMS - 1, ())
            for k in range(LAG):
                v_act(act, ITEMS - 1, SLOTS + k, False)
            finish_act(act, ITEMS - 1)

        @block.tensor
        def _(pe):
            def item(n, front, first=False):
                weave(front, lambda k: back_pe(pe, n, k, first), SLOTS)
            pe.wait_ge(s_boot, 6)
            alone(early_pe(pe, 0, False))
            alone(merge(mix_pe(pe, 0), early_pe(pe, 1)))
            item(0, merge(mix_pe(pe, 1), early_pe(pe, 2)), True)
            with pe.Fori(1, ITEMS - 2) as n:
                item(n, merge(mix_pe(pe, n + 1), early_pe(pe, n + 2)))
            item(ITEMS - 2, mix_pe(pe, ITEMS - 1))
            item(ITEMS - 1, ())
            for k in range(LAG):
                v_pe(pe, ITEMS - 1, SLOTS + k, True)


def kernel(**inputs):
    import numpy as np
    import concourse.bacc as bacc
    from concourse import mybir
    from concourse.bass_utils import run_bass_kernel_spmd as run

    a = {k: np.asarray(v) for k, v in inputs.items()}

    def tiles(v):
        return v.reshape(DEPTH, -1, P).transpose(0, 2, 1)

    conv = a["ssm_conv_w"].reshape(DEPTH, 4, 6, P).transpose(0, 3, 1, 2).reshape(DEPTH, P, 24)
    short = a["sc_conv_w"].reshape(DEPTH, 3, 2, P).transpose(0, 3, 1, 2).reshape(DEPTH, P, 6)
    item = np.arange(ITEMS)
    cst = np.stack([item % NB != 0, (item % NB) * P * BIG, (item // NB) * NEXP], -1).astype(np.float32)
    arrays = {
        "x": a["x"].reshape(SEQ, D),
        "w_in": a["w_in"].reshape(DEPTH, KT, P, IN_W).transpose(0, 2, 1, 3),
        "w_out": a["w_out"].reshape(DEPTH * D, D),
        "w_q": a["peer_w_q"].reshape(DEPTH, KT, P, KT, P).transpose(0, 3, 2, 1, 4).reshape(DEPTH * D, D),
        "keys": a["peer_sub_keys"].transpose(0, 3, 1, 2),
        "pk": np.concatenate([conv, tiles(a["ssm_conv_b"]), short, tiles(a["ssm_norm_w"])], -1),
        "rows": np.concatenate([a["ssm_dt_bias"], a["ssm_A_log"], a["ssm_D"]], -1),
        "norm2": a["norm2_w"],
        "fnorm": a["final_norm_w"].reshape(1, D),
        "norm1": tiles(a["norm1_w"]),
        "cst": np.broadcast_to(cst, (P, ITEMS, 3)),
        "peer_u": a["peer_u"].reshape(DEPTH * NEXP, D),
        "peer_v": a["peer_v"].reshape(DEPTH * NEXP, D),
    }
    arrays = {f"in_{k}": np.ascontiguousarray(v) for k, v in arrays.items()}
    nc = bacc.Bacc("TRN2", target_bir_lowering=False, num_devices=1)
    args = [nc.dram_tensor(k, v.shape, mybir.dt.from_np(v.dtype), kind="ExternalInput").ap()
            for k, v in arrays.items()]
    stream = nc.dram_tensor("stream", ((ITEMS + NB) * P, D), F32, kind="Internal").ap()
    out = nc.dram_tensor("out", (SEQ, D), F32, kind="ExternalOutput").ap()
    build(nc, *args, stream, out)
    result = run(nc, [arrays], core_ids=[0])
    return result.results[0]["out"].reshape(1, SEQ, D)
```
